# Optimizing a Trainium2 kernel written in Bass

```python
import math
import jax, jax.numpy as jnp
from jax import lax
import numpy as np

D_MODEL = 1024
BATCH = 1
SEQ = 256
DEPTH = 1
DEC_BATCH = 8
DEC_SEQ = 4
PAST_LEN = 2048
PAGE_SIZE = 128

D_MIX = D_MODEL
SSD_WIDTH = D_MIX // 2
SSD_HEAD_DIM = 64
SSD_HEADS = SSD_WIDTH // SSD_HEAD_DIM
SSD_GROUPS = 2
HEADS_PER_GROUP = SSD_HEADS // SSD_GROUPS
D_STATE = 128
CONV_W = 4
CONV_DIM = SSD_WIDTH + 2 * SSD_GROUPS * D_STATE
SSD_CHUNK = 128
MLP_WIDTH = D_MIX - SSD_WIDTH
MLP_HEADS = 8
MLP_HEAD_DIM = MLP_WIDTH // MLP_HEADS
MLP_CHUNK = 128
IN_DIM = SSD_WIDTH + CONV_DIM + SSD_HEADS + 2 * MLP_WIDTH
N_EXPERTS = 32
TOP_K = 4
D_FF = D_MODEL
SWIGLU_LIMIT = 7.0
SWIGLU_ALPHA = 1.702
MOE_BLOCK = 128
PLE_DIM = 256
EPS = 1e-6

kernel_name = "hymba_ssd_chunkmlp_moe_step"

def _rms(x):
    xf = x.astype(jnp.float32)
    return (xf * lax.rsqrt(jnp.mean(xf * xf, axis=-1, keepdims=True) + EPS)).astype(x.dtype)

def rmsnorm(x, g):
    return _rms(x) * g

def layernorm(x, g, b):
    xf = x.astype(jnp.float32)
    mu = jnp.mean(xf, axis=-1, keepdims=True)
    var = jnp.mean(jnp.square(xf - mu), axis=-1, keepdims=True)
    return ((xf - mu) * lax.rsqrt(var + EPS)).astype(x.dtype) * g + b

def ssd_chunked(x, dt, A, B, C, h0, q):
    b, l, h, p = x.shape
    c = l // q
    B = jnp.repeat(B, HEADS_PER_GROUP, axis=2)
    C = jnp.repeat(C, HEADS_PER_GROUP, axis=2)
    xdt = (x * dt[..., None]).reshape(b, c, q, h, p)
    Bc = B.reshape(b, c, q, h, -1)
    Cc = C.reshape(b, c, q, h, -1)
    a = (dt * A).reshape(b, c, q, h).transpose(0, 3, 1, 2)
    a_cum = jnp.cumsum(a, axis=-1)
    seg = a_cum[..., :, None] - a_cum[..., None, :]
    causal = jnp.tril(jnp.ones((q, q), dtype=bool))
    Lmat = jnp.exp(jnp.where(causal, seg, -jnp.inf))
    scores = jnp.einsum('bcihn,bcjhn->bhcij', Cc, Bc) * Lmat
    y_diag = jnp.einsum('bhcij,bcjhp->bcihp', scores, xdt)
    decay_states = jnp.exp(a_cum[..., -1:] - a_cum)
    states = jnp.einsum('bcjhn,bhcj,bcjhp->bchpn', Bc, decay_states, xdt)
    chunk_decay = jnp.exp(a_cum[..., -1])

    def step(h_prev, inp):
        st, dec = inp
        return h_prev * dec[..., None, None] + st, h_prev

    h_final, h_prev = lax.scan(step, h0, (states.transpose(1, 0, 2, 3, 4),
                                          chunk_decay.transpose(2, 0, 1)))
    y_off = jnp.einsum('bcihn,cbhpn,bhci->bcihp', Cc, h_prev, jnp.exp(a_cum))
    return (y_diag + y_off).reshape(b, l, h, p), h_final

def chunk_mix(v, w_s, b_s):
    bsz, l, _ = v.shape
    q = min(MLP_CHUNK, l)
    c = l // q
    vh = v.reshape(bsz, c, q, MLP_HEADS, MLP_HEAD_DIM)
    w = jnp.tril(w_s[:, :q, :q])
    s = jnp.einsum('hij,bcjhd->bcihd', w, vh) + b_s[:, :q].T[None, None, :, :, None]
    return s.reshape(bsz, l, MLP_WIDTH)

def token_mixers(a, conv_prev, ssm_prev, prm):
    bsz, l, _ = a.shape
    proj = a @ prm['w_in']
    o1 = SSD_WIDTH
    o2 = o1 + CONV_DIM
    o3 = o2 + SSD_HEADS
    o4 = o3 + MLP_WIDTH
    z, xbc, dt_raw, u, v = jnp.split(proj, [o1, o2, o3, o4], axis=-1)
    xpad = jnp.concatenate([conv_prev.astype(xbc.dtype), xbc], axis=1)
    conv = prm['conv_b'] + sum(prm['conv_w'][k] * xpad[:, k:k + l] for k in range(CONV_W))
    new_conv = xpad[:, l:]
    xbc = jax.nn.silu(conv)
    xs, bm, cm = jnp.split(xbc, [SSD_WIDTH, SSD_WIDTH + SSD_GROUPS * D_STATE], axis=-1)
    xs = xs.reshape(bsz, l, SSD_HEADS, SSD_HEAD_DIM).astype(jnp.float32)
    bm = bm.reshape(bsz, l, SSD_GROUPS, D_STATE).astype(jnp.float32)
    cm = cm.reshape(bsz, l, SSD_GROUPS, D_STATE).astype(jnp.float32)
    dt = jax.nn.softplus(dt_raw.astype(jnp.float32) + prm['dt_bias'].astype(jnp.float32))
    A = -jnp.exp(prm['a_log'].astype(jnp.float32))
    y, ssm_new = ssd_chunked(xs, dt, A, bm, cm, ssm_prev.astype(jnp.float32), min(SSD_CHUNK, l))
    y = y + prm['d_skip'].astype(jnp.float32)[:, None] * xs
    y = y.reshape(bsz, l, SSD_WIDTH).astype(a.dtype) * jax.nn.silu(z)
    y = _rms(y.reshape(bsz, l, SSD_GROUPS, SSD_WIDTH // SSD_GROUPS)).reshape(bsz, l, SSD_WIDTH) * prm['ssd_norm_g']
    u = jax.nn.gelu(u)
    v = layernorm(jax.nn.gelu(v), prm['v_norm_g'], prm['v_norm_b'])
    m = rmsnorm(u * chunk_mix(v, prm['w_spatial'], prm['b_spatial']), prm['mlp_out_g'])
    out = jnp.concatenate([y, m], axis=-1) @ prm['w_out']
    return out, new_conv, ssm_new.astype(ssm_prev.dtype), v

def moe(x, w_router, b_router, w_up, b_up, w_down, b_down):
    T, D = x.shape
    logits = x.astype(jnp.float32) @ w_router.astype(jnp.float32) + b_router.astype(jnp.float32)
    top_v, top_i = lax.top_k(logits, TOP_K)
    gates = jax.nn.softmax(top_v, axis=-1).astype(x.dtype)
    TK = T * TOP_K
    flat_e = top_i.reshape(TK)
    order = jnp.argsort(flat_e)
    sorted_e = flat_e[order]
    sorted_tok = (order // TOP_K).astype(jnp.int32)
    sorted_gate = gates.reshape(TK)[order]
    counts = jnp.bincount(flat_e, length=N_EXPERTS)
    start = jnp.cumsum(counts) - counts
    padded = (counts + MOE_BLOCK - 1) // MOE_BLOCK * MOE_BLOCK
    pend = jnp.cumsum(padded)
    pstart = pend - padded
    dest = pstart[sorted_e] + jnp.arange(TK) - start[sorted_e]
    n_blocks = -(-TK // MOE_BLOCK) + N_EXPERTS
    tok_buf = jnp.full((n_blocks * MOE_BLOCK,), T, jnp.int32).at[dest].set(sorted_tok)
    gate_buf = jnp.zeros((n_blocks * MOE_BLOCK,), x.dtype).at[dest].set(sorted_gate)
    block_e = jnp.clip(jnp.searchsorted(pend, jnp.arange(n_blocks) * MOE_BLOCK, side='right'), 0, N_EXPERTS - 1)
    x_pad = jnp.concatenate([x, jnp.zeros((1, D), x.dtype)], axis=0)

    def run_block(args):
        tok, g, e = args
        h = x_pad[tok] @ w_up[e] + b_up[e]
        gate = jnp.minimum(h[:, ::2], SWIGLU_LIMIT)
        lin = jnp.clip(h[:, 1::2], -SWIGLU_LIMIT, SWIGLU_LIMIT)
        act = gate * jax.nn.sigmoid(SWIGLU_ALPHA * gate) * (lin + 1)
        return (act @ w_down[e] + b_down[e]) * g[:, None]

    y_blocks = lax.map(run_block, (tok_buf.reshape(n_blocks, MOE_BLOCK),
                                   gate_buf.reshape(n_blocks, MOE_BLOCK), block_e))
    out = jnp.zeros((T + 1, D), x.dtype).at[tok_buf].add(y_blocks.reshape(-1, D))
    return out[:T]

def decoder_layer(h, p, conv_prev, ssm_prev, prm):
    mix, new_conv, new_ssm, v_rows = token_mixers(rmsnorm(h, prm['norm_mix_g']), conv_prev, ssm_prev, prm)
    h = h + mix
    m = rmsnorm(h, prm['norm_moe_g'])
    h = h + moe(m.reshape(-1, D_MODEL), prm['w_router'], prm['b_router'], prm['w_up'], prm['b_up'],
                prm['w_down'], prm['b_down']).reshape(h.shape)
    gate = jax.nn.sigmoid(rmsnorm(h, prm['norm_ple_g']) @ prm['w_ple_gate'])
    h = h + (p @ prm['w_ple_proj']) * gate
    return h, new_conv, new_ssm, v_rows

def setup_inputs(seed: int = 0) -> dict:
    key = jax.random.key(seed)
    ks = jax.random.split(key, 32)
    f = jnp.float32
    nrm = lambda k, shape, s: jax.random.normal(k, shape, f) * s
    dt0 = jnp.exp(jax.random.uniform(ks[10], (DEPTH, SSD_HEADS), f) * (math.log(0.1) - math.log(0.001)) + math.log(0.001))
    return {
        "x_prompt": nrm(ks[0], (BATCH, SEQ, D_MODEL), 1.0),
        "x_sample": nrm(ks[1], (DEC_BATCH, DEC_SEQ, D_MODEL), 1.0),
        "state_ssm": nrm(ks[2], (DEPTH, DEC_BATCH, SSD_HEADS, SSD_HEAD_DIM, D_STATE), 0.5),
        "state_conv": nrm(ks[3], (DEPTH, DEC_BATCH, CONV_W - 1, CONV_DIM), 1.0),
        "p_prompt": nrm(ks[4], (DEPTH, BATCH, SEQ, PLE_DIM), 1.0),
        "p_sample": nrm(ks[5], (DEPTH, DEC_BATCH, DEC_SEQ, PLE_DIM), 1.0),
        "norm_mix_g": 1.0 + nrm(ks[6], (DEPTH, D_MODEL), 0.02),
        "w_in": nrm(ks[7], (DEPTH, D_MODEL, IN_DIM), D_MODEL ** -0.5),
        "conv_w": nrm(ks[8], (DEPTH, CONV_W, CONV_DIM), CONV_W ** -0.5),
        "conv_b": nrm(ks[9], (DEPTH, CONV_DIM), 0.02),
        "dt_bias": dt0 + jnp.log(-jnp.expm1(-dt0)),
        "a_log": jnp.log(jax.random.uniform(ks[11], (DEPTH, SSD_HEADS), f, 1.0, 16.0)),
        "d_skip": 1.0 + nrm(ks[12], (DEPTH, SSD_HEADS), 0.1),
        "ssd_norm_g": 1.0 + nrm(ks[13], (DEPTH, SSD_WIDTH), 0.02),
        "v_norm_g": 1.0 + nrm(ks[14], (DEPTH, MLP_WIDTH), 0.02),
        "v_norm_b": nrm(ks[15], (DEPTH, MLP_WIDTH), 0.02),
        "w_spatial": nrm(ks[16], (DEPTH, MLP_HEADS, MLP_CHUNK, MLP_CHUNK), MLP_CHUNK ** -0.5),
        "b_spatial": 1.0 + nrm(ks[17], (DEPTH, MLP_HEADS, MLP_CHUNK), 0.02),
        "mlp_out_g": 1.0 + nrm(ks[18], (DEPTH, MLP_WIDTH), 0.02),
        "w_out": nrm(ks[19], (DEPTH, D_MIX, D_MODEL), D_MIX ** -0.5),
        "norm_moe_g": 1.0 + nrm(ks[20], (DEPTH, D_MODEL), 0.02),
        "w_router": nrm(ks[21], (DEPTH, D_MODEL, N_EXPERTS), D_MODEL ** -0.5),
        "b_router": nrm(ks[22], (DEPTH, N_EXPERTS), 0.01),
        "w_up": nrm(ks[23], (DEPTH, N_EXPERTS, D_MODEL, 2 * D_FF), D_MODEL ** -0.5),
        "b_up": nrm(ks[24], (DEPTH, N_EXPERTS, 2 * D_FF), 0.02),
        "w_down": nrm(ks[25], (DEPTH, N_EXPERTS, D_FF, D_MODEL), D_FF ** -0.5),
        "b_down": nrm(ks[26], (DEPTH, N_EXPERTS, D_MODEL), 0.02),
        "norm_ple_g": 1.0 + nrm(ks[27], (DEPTH, D_MODEL), 0.02),
        "w_ple_gate": nrm(ks[28], (DEPTH, D_MODEL, D_MODEL), D_MODEL ** -0.5),
        "w_ple_proj": nrm(ks[29], (DEPTH, PLE_DIM, D_MODEL), PLE_DIM ** -0.5),
        "norm_final_g": 1.0 + nrm(ks[30], (D_MODEL,), 0.02),
    }

def reference(x_prompt, x_sample, state_ssm, state_conv, p_prompt, p_sample,
              norm_mix_g, w_in, conv_w, conv_b, dt_bias, a_log, d_skip, ssd_norm_g,
              v_norm_g, v_norm_b, w_spatial, b_spatial, mlp_out_g, w_out,
              norm_moe_g, w_router, b_router, w_up, b_up, w_down, b_down,
              norm_ple_g, w_ple_gate, w_ple_proj, norm_final_g):
    hp, hs = x_prompt, x_sample
    bp = x_prompt.shape[0]
    ssm_p, conv_p, ssm_s, conv_s, v_s = [], [], [], [], []
    for i in range(DEPTH):
        prm = {
            'norm_mix_g': norm_mix_g[i], 'w_in': w_in[i], 'conv_w': conv_w[i], 'conv_b': conv_b[i],
            'dt_bias': dt_bias[i], 'a_log': a_log[i], 'd_skip': d_skip[i], 'ssd_norm_g': ssd_norm_g[i],
            'v_norm_g': v_norm_g[i], 'v_norm_b': v_norm_b[i], 'w_spatial': w_spatial[i],
            'b_spatial': b_spatial[i], 'mlp_out_g': mlp_out_g[i], 'w_out': w_out[i],
            'norm_moe_g': norm_moe_g[i], 'w_router': w_router[i], 'b_router': b_router[i],
            'w_up': w_up[i], 'b_up': b_up[i], 'w_down': w_down[i], 'b_down': b_down[i],
            'norm_ple_g': norm_ple_g[i], 'w_ple_gate': w_ple_gate[i], 'w_ple_proj': w_ple_proj[i],
        }
        conv0 = jnp.zeros((bp, CONV_W - 1, CONV_DIM), x_prompt.dtype)
        ssm0 = jnp.zeros((bp, SSD_HEADS, SSD_HEAD_DIM, D_STATE), state_ssm.dtype)
        hp, cp, sp, _ = decoder_layer(hp, p_prompt[i], conv0, ssm0, prm)
        hs, cs, ss, vs = decoder_layer(hs, p_sample[i], state_conv[i], state_ssm[i], prm)
        ssm_p.append(sp)
        conv_p.append(cp)
        ssm_s.append(ss)
        conv_s.append(cs)
        v_s.append(vs)
    y_prompt = rmsnorm(hp, norm_final_g)
    y_sample = rmsnorm(hs, norm_final_g)
    new_ssm_prompt = jnp.stack(ssm_p)
    new_conv_prompt = jnp.stack(conv_p)
    new_ssm_sample = jnp.stack(ssm_s)
    new_conv_sample = jnp.stack(conv_s)
    new_chunk_v_sample = jnp.stack(v_s)
    return (y_prompt, y_sample, new_ssm_prompt, new_conv_prompt, new_ssm_sample, new_conv_sample, new_chunk_v_sample)


_drawn_inputs = setup_inputs


def setup_inputs(seed=0):
    import zlib

    import numpy as np

    out = dict(_drawn_inputs(seed))
    spreads = {}
    factors = {'v_norm_g': 8.72,
     'v_norm_b': 7.72,
     'b_up': 7.128,
     'b_down': 8.0,
     'norm_ple_g': 162.569,
     'norm_final_g': 20.991,
     'b_router': 3.486,
     'b_spatial': 3.25}
    for name, (base, spread) in spreads.items():
        noise = np.random.default_rng([zlib.crc32(name.encode()), seed]).standard_normal(out[name].shape)
        drawn = base * np.exp(spread * noise) if base else spread * noise
        out[name] = __import__('jax').numpy.asarray(drawn.astype(out[name].dtype))
    for name, factor in factors.items():
        out[name] = (out[name] * factor).astype(out[name].dtype)
    return out
```

```python
from contextlib import ExitStack

import concourse.bass as bass
from concourse import mybir

ALU = mybir.AluOpType
ACT = mybir.ActivationFunctionType
AX_X = mybir.AxisListType.X
F32 = mybir.dt.float32
BF16 = mybir.dt.bfloat16
I32 = mybir.dt.int32

P = 128
D = 1024
KD = D // P
T_PROMPT, B_S, L_S = 256, 8, 4
T_S = B_S * L_S
T = T_PROMPT + T_S
ROWS = [128, 128, T_S]
TOK = [slice(0, 128), slice(128, 256), slice(256, T)]
NCH = 3
SSD, HEADS, HD, GROUPS, HPG, N_ST = 512, 8, 64, 2, 4, 128
CONV = 1024
MLP, MHEADS, MHD = 512, 8, 64
NE, TOPK, FF = 32, 4, 1024
PLE = 256
CAP = 64
PASSES = -(-T // CAP)
NCOL = PASSES * NE + 2
LIMIT, ALPHA, EPS = 7.0, 1.702, 1e-6
NEG = -1e30
BIG = 3e38


def plan_psum():
    both = [(c, hf) for c in range(NCH) for hf in range(2)]
    jobs = [("par", 2, None)]
    jobs += [(("xT", *ch), 1, None) for ch in both]
    jobs += [("dt", 3, None)]
    jobs += [(("xbc", t), 2, None) for t in range(8)]
    jobs += [((n, hf), 1, None) for n in ("cvp", "cvs") for hf in range(2)]
    jobs += [((n, c), 1, None) for n in "zuv" for c in range(NCH)]
    jobs += [("acum", 2, None)]
    jobs += [(("acb", c, g), 5, None) for c in range(2) for g in range(GROUPS)] + [("acb2", 8, None)]
    jobs += [(("wT", q), 1, None) for q in range(2)] + [("bT", 1, None), ("rep", 2, None)]
    jobs += [((n, c), 1, None) for c in range(NCH) for n in ("xtm", "btm")]
    jobs += [(("cb", c), 2, None) for c in range(NCH)]
    jobs += [(("st", c), 1, None) for c in range(2)]
    jobs += [(("yd", 0), 1, 0), (("yd", 1), 1, 1), ("yo1", 1, 2), (("yd", 2), 1, 3)]
    jobs += [(("yos", g), 1, 6 + g) for g in range(GROUPS)]
    jobs += [(("h0T", b), 1, b % 6) for b in range(B_S)]
    jobs += [("decs", 1, None), ("hf", 1, None)]
    jobs += [(("sp", c), 1, None) for c in range(NCH)]
    jobs += [(("cat", c, hf), 1, None) for hf in range(2) for c in range(NCH)]
    jobs += [(("ns", t, b), 4, None) for t in range(4) for b in range(2)]
    jobs += [(("wo", *ch), 1, None) for ch in both]
    jobs += [(("mT", *ch), 1, None) for ch in both]
    jobs += [("lg", 3, None), ("pos", 4, None), ("gT", 1, None)]
    jobs += [(("bd", *ch), 1, None) for ch in both]
    jobs += [("end_moe", 0, None)]
    jobs += [(("pT", k), 1, None) for k in range(2)]
    jobs += [(("pp", *ch), 1, None) for ch in both]
    jobs += [(("nT", *ch), 1, None) for ch in both]
    jobs += [(("pg", *ch), 1, None) for ch in both]
    place, full, free, turn = {}, [0] * 8, [0] * 8, 0
    for name, reads, bank in jobs:
        if name == "end_moe":
            place[name] = (list(full), list(free))
            continue
        if bank is None:
            bank, turn = turn % 8, turn + 1
        place[name] = (bank, full[bank] + 1, free[bank], free[bank] + reads)
        full[bank] += 1
        free[bank] += reads
    return place


def build(nc, I, O):
    PS = plan_psum()
    ctx = ExitStack()
    with ctx:
        def sb(name, shape, dt=F32):
            return ctx.enter_context(nc.sbuf_tensor(name, shape, dt))

        def semaphores(text):
            return {n: ctx.enter_context(nc.semaphore(n)) for n in text.split()}

        ring = sb("ring", [P, 12 * 2048])
        h = sb("h", [P, NCH, D])
        aT = sb("aT", [P, KD, T])
        arena = sb("arena", [P, 21760])
        ident, upper, strict, ones, negm = (sb(n, [P, P]) for n in ("ident", "upper", "strict", "ones", "negm"))
        upper_s, block_s, negm_s = (sb(n, [T_S, T_S]) for n in ("upper_s", "block_s", "negm_s"))
        seq_s = sb("seq_s", [T_S, B_S])
        rep4 = sb("rep4", [L_S, T_S])
        iota = sb("iota", [P, CAP])
        bias_ones = sb("bias_ones", [P, CAP], BF16)
        thr = sb("thr", [1, PASSES - 1])
        pf = sb("pf", [P, KD, 9])
        pb = sb("pb", [P, 3 * HEADS])
        brow = sb("brow", [P, NE])
        small = sb("small", [P, 12, NCH * HEADS])
        stat = sb("stat", [P, 11, NCH])
        gstat = sb("gstat", [P, 2, 2 * NCH])
        bn = sb("bn", [P, NCH, 6])
        mv = sb("mv", [P, NCH, 2])
        eps = sb("eps", [P, 1])
        bsp = sb("bsp", [P, MHEADS])
        bss = sb("bss", [T_S, MHEADS])
        decs = sb("decs", [P, 4, B_S])
        npf = sb("npf", [1, 8])
        npi = sb("npi", [1, 1], I32)

        dtr, dta, dtb, dtc, dt, av, acum, atot, eac, dec = (
            small[:, n, :].rearrange("p (c h) -> p c h", c=NCH) for n in range(10))
        aneg = small[:, 10, 0:HEADS]
        edec = small[:, 11, 0:HEADS]
        ss_x, rs_x, ss_m, rs_m, ss_o, rs_o, ss_p, rs_p, ss_f, rs_f, rs_v = (stat[:, n, :] for n in range(11))
        ss_g, rs_g = gstat[:, 0, :], gstat[:, 1, :]

        def view(at, *dims):
            n = 1
            for x in dims:
                n *= x
            v = arena[:, at:at + n]
            names = "abcd"[:len(dims)]
            return v.rearrange("p (%s) -> p %s" % (" ".join(names), " ".join(names)),
                               **dict(zip(names, dims))) if len(dims) > 1 else v

        xact = view(0, KD, T)
        zs, us, vs = view(2304, NCH, SSD), view(3840, NCH, MLP), view(5376, NCH, MLP)
        xs, xdt = view(6912, NCH, SSD), view(8448, NCH, SSD)
        xn = view(6912, NCH, D)
        xdtd = view(9984, NCH, SSD)
        cvp = view(9984, 1024)
        junk_x = view(9984, 1024)
        btm = view(11520, NCH, 2, N_ST)
        bmask = view(12288, GROUPS, B_S, N_ST)
        cmask = view(14336, GROUPS, B_S, T_S)
        xp = view(12288, KD, T_PROMPT + 3)
        xps = view(12288 + KD * (T_PROMPT + 3), KD, L_S + 3, B_S)
        hs1, hs2 = view(14848, SSD), view(15360, SSD)
        wsp = view(14848, MHEADS, P)
        h0t = view(15872, 2, SSD)
        prow = view(15872, 1024)
        wspT = view(16896, MHEADS, P)
        wsps = view(17920, MHEADS, B_S, L_S)
        vgb = view(18176, 2, MLP)
        bup_f, bup_r = view(19200, 512), view(19712, 512)
        bup_p = view(20224, 768).bitcast(BF16).rearrange("p (t n) -> p t n", t=3)
        cvs = view(19200, 1024)
        aex = view(20224, 512)
        wrt = view(20992, KD, NE)
        junk = view(19200, 512)
        seqm = view(21504, B_S, T_S)
        bsn = view(11008, P)
        lmat = aT[:, :, :].rearrange("p k t -> p (k t)")[:, 0:2048].rearrange("p (c h i) -> p c h i", c=2, h=HEADS)
        lmat_s = aT[:, :, :].rearrange("p k t -> p (k t)")[0:T_S, 2048:2304].rearrange("p (h i) -> p h i", h=HEADS)
        mbf = view(0, 4608).bitcast(BF16).rearrange("p (c t n) -> p c t n", c=NCH, t=3)
        mn = view(4608, NCH, D)
        mr = view(7680, NCH, D)
        xT = view(7680, 2, KD, CAP)
        sg, sl, sq = view(8704, 512), view(9216, 512), view(9728, 512)
        act_h = view(10240, 512)
        actT = view(10752, 4, 2, CAP)
        ysb = view(11264, D)
        gsel = view(12288, NCH, P)
        gselT = view(12672, T)
        sel = view(12960, 192).bitcast(BF16).rearrange("p (x c s) -> p x c s", x=2, c=NCH)
        bias = view(13152, 1024).bitcast(BF16)
        pos_t, gate_t = view(14176, NCH, NCOL), view(14662, NCH, NCOL)
        bdn = view(15404, 1024)
        gT = view(16428, T)
        lgt = view(16716, NCH, 40)
        mrep, msk, gat, ex, prk = (view(16836 + 128 * n, NCH, 40) for n in range(5))
        top8, top4 = view(17480, NCH, 8), view(17504, NCH, 8)
        gsum, grec = view(17528, NCH), view(17532, NCH)
        pp = view(17536, NCH, D)
        pgs = view(0, NCH, D)
        hn = view(4608, NCH, D)
        gfin = view(7680, D)
        prows = view(8704, NCH, PLE)
        pT = view(9472, 2, T)
        yout = view(10240, NCH, D)

        w_xbc = ring[:, 0:8192].rearrange("p (k n) -> p k n", k=KD)
        w_zuv = [ring[:, 8192 + 4096 * n:12288 + 4096 * n].rearrange("p (k n) -> p k n", k=KD) for n in range(3)]
        w_o = ring[:, 0:8192].rearrange("p (k n) -> p k n", k=KD)
        w_dt = ring[:, 20480:20544].rearrange("p (k n) -> p k n", k=KD)
        h0 = ring[:, 20480:24576].rearrange("p (b t n) -> p b t n", b=B_S, t=4)
        w_pg = ring[:, 0:8192].rearrange("p (k n) -> p k n", k=KD)
        w_pp = ring[:, 8192:10240].rearrange("p (k n) -> p k n", k=2)

        def slot(s):
            return ring[:, 2048 * s:2048 * (s + 1)]

        bank = [ctx.enter_context(nc.psum_tensor(f"bank{b}", [P, 512], F32)) for b in range(8)]
        bup_split = nc.dram_tensor("bup_split", [3, NE, 2 * FF], BF16, kind="Internal").ap()

        bank_full = [ctx.enter_context(nc.semaphore(f"bank_full{b}")) for b in range(8)]
        bank_free = [ctx.enter_context(nc.semaphore(f"bank_free{b}")) for b in range(8)]
        S = semaphores(
            "aex_ok a_ok ach act_ready anexp at_free at_full bdn_in bias_in bias_zero bmask_ok brow_in bs_in bup_in "
            "bup_parts bup_stored cmask_ok consts conv_ok cv_out dec_in dt dt_in dtabs dtadd dtexp dtln "
            "eac_ok end_moe fin_ss fss g_ok g_ready gates_ok gex gf_in gl_ok h0_in h0t_used hf_out hfin "
            "hn_ok hss ident_ok lexp m1_ok m2_ok m3_ok m_ok mask_ok mbf_zero mix_done mix_ok mn_ok moe_done "
            "mss ngm_ok npass_ok ns_out pads par_in pb_in pch pr_in pw_in r1_ok rs_f_ok rs_g_ok rs_m_ok "
            "rs_o_ok rs_p_ok rstd_x rsv rsv_in sel_ok sig_ready sumsq u_in up_free up_full v_in v_out vch "
            "vgb_in vinit vn_ok w_used wmask wo_in wrt_in wsp_in x_in xact_ok xbc_in xdtd_ok xn_ok xt_full "
            "xt_ready y_full y_ok y_out ygs yn_ok yo_ok ysb_ok z_in")
        w_full = [ctx.enter_context(nc.semaphore(f"w_full{s}")) for s in range(12)]
        s_full = [ctx.enter_context(nc.semaphore(f"s_full{s}")) for s in range(3)]
        s_free = [ctx.enter_context(nc.semaphore(f"s_free{s}")) for s in range(3)]

        def filled(eng, name):
            b, full, _, _ = PS[name]
            eng.wait_ge(bank_full[b], full)
            return bank[b]

        def stored(eng, name):
            b, _, _, after = PS[name]
            eng.wait_ge(bank_free[b], after)

        def freed(name):
            return bank_free[PS[name][0]]

        BANK_END = PS["end_moe"]
        N_CONST = 9

        CH = [(c, hf) for c in range(NCH) for hf in range(2)]
        hs3 = lambda ap: ap.rearrange("p (h d) -> p h d", d=HD)

        def over(ap, shape):
            return ap.unsqueeze(2).to_broadcast(shape)

        block = ctx.enter_context(nc.Block())

        @block.sync
        def _(sp):
            xr = I["x_prompt"].rearrange("a (c p) d -> p (a c) d", p=P)
            sp.dma_start(h[:, 0, :], xr[:, 0, :]).then_inc(S["x_in"], 16)
            sp.dma_start(h[:, 1, :], xr[:, 1, :]).then_inc(S["x_in"], 16)
            sp.dma_start(h[0:T_S, 2, :], I["x_sample"].rearrange("b s d -> (b s) d")).then_inc(S["x_in"], 16)
            w_in = I["w_in"][0].rearrange("(k p) n -> p k n", p=P)
            o = SSD + CONV
            with nc.allow_non_contiguous_dma(reason="eight dt columns"):
                sp.dma_start(w_dt, w_in[:, :, o:o + HEADS]).then_inc(S["dt_in"], 16)
            for q in range(2):
                sp.dma_start(w_xbc[:, 4 * q:4 * q + 4, :], w_in[:, 4 * q:4 * q + 4, SSD:o]).then_inc(S["xbc_in"], 16)
            sp.dma_start(w_zuv[0], w_in[:, :, 0:SSD]).then_inc(S["z_in"], 16)
            sp.dma_start(w_zuv[1], w_in[:, :, o + HEADS:o + HEADS + MLP]).then_inc(S["u_in"], 16)
            sp.dma_start(w_zuv[2], w_in[:, :, o + HEADS + MLP:o + HEADS + 2 * MLP]).then_inc(S["v_in"], 16)
            b, full, _, _ = PS["dt"]
            sp.wait_ge(bank_full[b], full)
            sp.dma_start(h0, I["state_ssm"][0].rearrange("b h q n -> b (h q) n").rearrange("b (t p) n -> p b t n", p=P))\
              .then_inc(S["h0_in"], 16)
            b, full, _, _ = PS[("xbc", 7)]
            sp.wait_ge(bank_full[b], full)
            sp.dma_start(w_o, I["w_out"][0].rearrange("(k p) n -> p k n", p=P)).then_inc(S["wo_in"], 16)

            def up_tile(e, s):
                return I["w_up"][0, e, s * P:(s + 1) * P, :]

            def down_tile(e, s):
                return I["w_down"][0, e, 2 * s * P:(2 * s + 2) * P, :].rearrange("(a p) n -> p a n", p=P)

            order = [4, 5, 6, 7, 8, 9, 0, 1, 2, 3, 10, 11]
            behind = {4: ("z", 2), 6: ("u", 2), 8: ("v", 2), 0: ("wo", 2, 1)}
            for s in order:
                if s in behind:
                    b, full, _, _ = PS[behind[s]]
                    sp.wait_ge(bank_full[b], full)
                if s == 10:
                    sp.wait_ge(S["ns_out"], 16)
                if s < 8:
                    sp.dma_start(slot(s), up_tile(0, s)).then_inc(w_full[s], 16)
                else:
                    sp.dma_start(slot(s).rearrange("p (a n) -> p a n", a=2), down_tile(0, s - 8)).then_inc(w_full[s], 16)
            sp.wait_ge(S["bup_stored"], 16)
            sp.wait_ge(S["bias_zero"], 1)

            def fetch_bias(e):
                sp.dma_start(bias[0:3, :], bup_split[:, bass.ds(e, 1), :].rearrange("t a n -> (t a) n"))\
                  .then_inc(S["bias_in"], 16)

            fetch_bias(0)

            def fetch(i, e):
                for s in range(12):
                    if s == 7:
                        sp.wait_ge(S["up_full"], 2 * i)
                    elif s == 11:
                        sp.wait_ge(S["y_full"], i + 1)
                    else:
                        sp.wait_ge(S["w_used"], 10 * i - 10 + s + 1 - (s > 7))
                    if s == 0:
                        fetch_bias(e)
                    if s < 8:
                        src = I["w_up"][0, bass.ds(e, 1), s * P:(s + 1) * P, :].rearrange("a p n -> (a p) n")
                        sp.dma_start(slot(s), src).then_inc(w_full[s], 16)
                    else:
                        q = s - 8
                        src = I["w_down"][0, bass.ds(e, 1), 2 * q * P:(2 * q + 2) * P, :]
                        sp.dma_start(slot(s).rearrange("p (a n) -> p a n", a=2),
                                     src.rearrange("e (a p) n -> p (e a) n", p=P)).then_inc(w_full[s], 16)

            with sp.Fori(1, NE) as e:
                fetch(e, e)
            sp.wait_ge(S["npass_ok"], 1)
            n_pass = sp.value_load(npi[0:1, 0:1], min_val=1, max_val=PASSES)
            with sp.If(n_pass > 1):
                with sp.Fori(1, n_pass) as r:
                    with sp.Fori(0, NE) as e:
                        fetch(r * NE + e, e)
            sp.wait_ge(S["up_full"], n_pass * (2 * NE))
            wpg = I["w_ple_gate"][0].rearrange("(k p) n -> p k n", p=P)
            for q in range(2):
                sp.dma_start(w_pg[:, 4 * q:4 * q + 4, :], wpg[:, 4 * q:4 * q + 4, :]).then_inc(S["pw_in"], 16)
            sp.dma_start(w_pp, I["w_ple_proj"][0].rearrange("(k p) n -> p k n", p=P)).then_inc(S["pw_in"], 16)
            sp.wait_ge(S["moe_done"], 1)
            sp.dma_start(gfin, I["norm_final_g"].partition_broadcast(P)).then_inc(S["gf_in"], 16)
            ypr = O["y_prompt"].rearrange("a (c p) d -> p (a c) d", p=P)
            for c in range(NCH):
                sp.wait_ge(S["yo_ok"], c + 1)
                if c < 2:
                    sp.dma_start(ypr[:, c, :], yout[:, c, :]).then_inc(S["y_out"], 16)
                else:
                    sp.dma_start(O["y_sample"].rearrange("b s d -> (b s) d"), yout[0:T_S, 2, :]).then_inc(S["y_out"], 16)
            sp.wait_ge(S["y_out"], 16 * NCH)

        @block.gpsimd
        def _(pool):
            n_done = [0]

            def step(ins):
                n_done[0] += 1
                ins.then_inc(S["pch"], 1)
                pool.wait_ge(S["pch"], n_done[0])

            pool.dma_start(pb[:, 0:HEADS], I["dt_bias"][0].partition_broadcast(P)).then_inc(S["pb_in"], 16)
            pool.dma_start(pb[:, HEADS:2 * HEADS], I["a_log"][0].partition_broadcast(P)).then_inc(S["pb_in"], 16)
            pool.dma_start(pb[:, 2 * HEADS:], I["d_skip"][0].partition_broadcast(P)).then_inc(S["pb_in"], 16)
            step(pool.memset(ident[:, :], 0.0))
            pool.affine_select(out=ident[:, :], in_=ident[:, :], compare_op=ALU.not_equal, fill=1.0,
                               base=0, pattern=[[-1, P]], channel_multiplier=1).then_inc(S["ident_ok"], 1)
            pool.memset(xp[:, :, 0:3], 0.0).then_inc(S["pads"], 1)
            step(pool.memset(ones[:, :], 1.0))
            pool.affine_select(out=upper[:, :], in_=ones[:, :], compare_op=ALU.is_ge, fill=0.0,
                               base=0, pattern=[[1, P]], channel_multiplier=-1).then_inc(S["consts"], 1)
            pool.affine_select(out=strict[:, :], in_=ones[:, :], compare_op=ALU.is_ge, fill=0.0,
                               base=-1, pattern=[[1, P]], channel_multiplier=-1).then_inc(S["consts"], 1)
            step(pool.memset(negm[:, :], 0.0))
            pool.affine_select(out=negm[:, :], in_=negm[:, :], compare_op=ALU.is_ge, fill=NEG,
                               base=0, pattern=[[1, P]], channel_multiplier=-1).then_inc(S["consts"], 1)
            bb = block_s[:, :].rearrange("p (b s) -> p b s", b=B_S)
            one_s = ones[0:T_S, 0:T_S].rearrange("p (b s) -> p b s", b=B_S)
            step(pool.affine_select(out=bb, in_=one_s, compare_op=ALU.is_ge, fill=0.0, base=0,
                                    pattern=[[-L_S, B_S], [0, L_S]], channel_multiplier=1))
            step(pool.affine_select(out=bb, in_=bb, compare_op=ALU.is_ge, fill=0.0, base=L_S - 1,
                                    pattern=[[L_S, B_S], [0, L_S]], channel_multiplier=-1))
            step(pool.affine_select(out=upper_s[:, :], in_=block_s[:, :], compare_op=ALU.is_ge, fill=0.0,
                                    base=0, pattern=[[1, T_S]], channel_multiplier=-1))
            pool.tensor_scalar(negm_s[:, :], upper_s[:, :], -1.0, -NEG, ALU.add, ALU.mult).then_inc(S["consts"], 1)
            step(pool.affine_select(out=seq_s[:, :], in_=ones[0:T_S, 0:B_S], compare_op=ALU.is_ge, fill=0.0, base=0,
                                    pattern=[[-L_S, B_S]], channel_multiplier=1))
            pool.affine_select(out=seq_s[:, :], in_=seq_s[:, :], compare_op=ALU.is_ge, fill=0.0, base=L_S - 1,
                               pattern=[[L_S, B_S]], channel_multiplier=-1).then_inc(S["consts"], 1)
            step(pool.memset(rep4[:, :], 0.0))
            r4 = rep4[:, :].rearrange("p (b s) -> p b s", b=B_S)
            pool.affine_select(out=r4, in_=r4, compare_op=ALU.not_equal, fill=1.0, base=0,
                               pattern=[[0, B_S], [1, L_S]], channel_multiplier=-1).then_inc(S["consts"], 1)
            pool.iota(iota[:, :], pattern=[[1, CAP]], base=0, channel_multiplier=0,
                      allow_small_or_imprecise_dtypes=True).then_inc(S["consts"], 1)
            pool.iota(thr[:, :], pattern=[[CAP, PASSES - 1]], base=CAP, channel_multiplier=0,
                      allow_small_or_imprecise_dtypes=True).then_inc(S["consts"], 1)
            one_m = ones[:, 0:T_S].unsqueeze(1).to_broadcast([P, B_S, T_S])
            step(pool.affine_select(out=seqm, in_=one_m, compare_op=ALU.is_ge, fill=0.0, base=0,
                                    pattern=[[-L_S, B_S], [1, T_S]], channel_multiplier=0))
            pool.affine_select(out=seqm, in_=seqm, compare_op=ALU.is_ge, fill=0.0, base=L_S - 1,
                               pattern=[[L_S, B_S], [-1, T_S]], channel_multiplier=0).then_inc(S["consts"], 1)
            pool.wait_ge(S["wsp_in"], 16)
            pool.affine_select(out=wsp, in_=wsp, compare_op=ALU.is_ge, fill=0.0, base=0,
                               pattern=[[0, MHEADS], [-1, P]], channel_multiplier=1).then_inc(S["wmask"], 1)
            pool.wait_ge(S["bup_in"], 16)
            step(pool.tensor_copy(bup_p[:, 0, :], bup_f))
            step(pool.tensor_tensor(bup_r, bup_f, bup_p[:, 0, :], ALU.subtract))
            step(pool.tensor_copy(bup_p[:, 1, :], bup_r))
            step(pool.tensor_tensor(bup_f, bup_r, bup_p[:, 1, :], ALU.subtract))
            pool.tensor_copy(bup_p[:, 2, :], bup_f).then_inc(S["bup_parts"], 1)
            pool.wait_ge(S["bup_parts"], 1)
            pool.dma_start(bup_split.rearrange("t e (q n) -> (e q) t n", n=512), bup_p).then_inc(S["bup_stored"], 16)
            for n in ("cvp", "cvs"):
                for hf in range(2):
                    stored(pool, (n, hf))
            pool.dma_start(O["new_conv_prompt"][0, 0], cvp[T_S - 3:T_S, :]).then_inc(S["cv_out"], 16)
            for t in range(1, L_S):
                pool.dma_start(O["new_conv_sample"][0, :, t - 1, :], cvs[B_S * t:B_S * t + B_S, :]).then_inc(S["cv_out"], 16)
            pool.wait_ge(S["cv_out"], 16 * L_S)
            pool.wait_ge(S["vn_ok"], 3)
            pool.dma_start(O["new_chunk_v_sample"][0].rearrange("b s d -> (b s) d"), vs[0:T_S, 2, :])\
                .then_inc(S["v_out"], 16)
            stored(pool, "hf")
            pool.dma_start(O["new_ssm_prompt"][0, 0].rearrange("h q n -> (h q) n").rearrange("(t p) n -> p t n", p=P),
                           xdt[:, 0, :].rearrange("p (t n) -> p t n", t=4)).then_inc(S["hf_out"], 16)
            for t in range(4):
                for bh in range(2):
                    stored(pool, ("ns", t, bh))
            pool.dma_start(O["new_ssm_sample"][0].rearrange("b h q n -> b (h q) n").rearrange("b (t p) n -> p b t n", p=P),
                           h0).then_inc(S["ns_out"], 16)
            pool.wait_ge(S["v_out"], 16)
            pool.wait_ge(S["hf_out"], 16)
            pool.wait_ge(S["ns_out"], 16)
            pool.wait_ge(S["mix_done"], 1)
            pool.dma_start(bdn[0:NE, :], I["b_down"][0]).then_inc(S["bdn_in"], 16)
            pool.wait_ge(S["moe_done"], 1)
            pq = I["p_prompt"][0].rearrange("a (c p) d -> p (a c) d", p=P)
            pool.dma_start(prows[:, 0:2, :], pq).then_inc(S["pr_in"], 16)
            pool.dma_start(prows[0:T_S, 2, :], I["p_sample"][0].rearrange("b s d -> (b s) d")).then_inc(S["pr_in"], 16)

        @block.tensor
        def _(pe):
            def open_bank(name):
                b, _, before, _ = PS[name]
                if before:
                    pe.wait_ge(bank_free[b], before)
                return bank[b]

            def close_bank(name, mm):
                mm.then_inc(bank_full[PS[name][0]], 1)

            pe.wait_ge(S["ident_ok"], 1)
            pe.wait_ge(S["par_in"], 16 * 8)
            o = open_bank("par")
            for k in range(KD):
                mm = pe.transpose(o[:, 33 * k:33 * k + 33], prow[0:33, k * P:(k + 1) * P], ident[0:33, 0:33])
            close_bank("par", mm)

            def transposed(tag, src, ready, order):
                for c, hf in order:
                    pe.wait_ge(S[ready], c + 1)
                    o = open_bank((tag, c, hf))
                    for j in range(4):
                        k = 4 * hf + j
                        mm = pe.transpose(o[:, j * ROWS[c]:(j + 1) * ROWS[c]], src[0:ROWS[c], c, k * P:(k + 1) * P],
                                          ident[0:ROWS[c], 0:ROWS[c]])
                    close_bank((tag, c, hf), mm)

            transposed("xT", xn, "xn_ok", CH)

            for ch in CH:
                stored(pe, ("xT", *ch))
            pe.wait_ge(S["dt_in"], 16)
            o = open_bank("dt")
            for c in range(NCH):
                for k in range(KD):
                    mm = pe.matmul(o[0:ROWS[c], 8 * c:8 * c + 8], aT[:, k, TOK[c]], w_dt[:, k, :],
                                   start=(k == 0), stop=(k == KD - 1))
            close_bank("dt", mm)
            for t in range(8):
                if t == 0:
                    pe.wait_ge(S["xbc_in"], 32)
                o = open_bank(("xbc", t))
                for k in range(KD):
                    mm = pe.matmul(o[:, 0:T], w_xbc[:, k, t * P:(t + 1) * P], aT[:, k, :],
                                   start=(k == 0), stop=(k == KD - 1))
                close_bank(("xbc", t), mm)
            for t in range(8):
                stored(pe, ("xbc", t))
            for n in ("cvp", "cvs"):
                for hf in range(2):
                    o = open_bank((n, hf))
                    for j in range(4):
                        k = 4 * hf + j
                        src = xp[:, k, T_PROMPT + 3 - T_S:T_PROMPT + 3] if n == "cvp" else xps[:, k, 3:L_S + 3, :].rearrange("p s b -> p (s b)")
                        mm = pe.transpose(o[0:T_S, j * P:(j + 1) * P], src, ident[:, :])
                    close_bank((n, hf), mm)

            def project(tag, n, ready):
                pe.wait_ge(S[ready], 16)
                for c in range(NCH):
                    o = open_bank((tag, c))
                    for k in range(KD):
                        mm = pe.matmul(o[0:ROWS[c], :], aT[:, k, TOK[c]], w_zuv[n][:, k, :],
                                       start=(k == 0), stop=(k == KD - 1))
                    close_bank((tag, c), mm)

            project("z", 0, "z_in")
            project("u", 1, "u_in")
            project("v", 2, "v_in")

            pe.wait_ge(S["a_ok"], 1)
            pe.wait_ge(S["consts"], N_CONST)
            o = open_bank("acum")
            for c in range(2):
                pe.matmul(o[:, 8 * c:8 * c + 8], upper[:, :], av[:, c, :], start=True, stop=True)
            pe.matmul(o[0:T_S, 16:24], upper_s[:, :], av[0:T_S, 2, :], start=True, stop=True)
            mm = pe.matmul(o[0:T_S, 24:32], block_s[:, :], av[0:T_S, 2, :], start=True, stop=True)
            close_bank("acum", mm)
            for c in range(2):
                for g in range(GROUPS):
                    o = open_bank(("acb", c, g))
                    for j in range(HPG):
                        hh = HPG * g + j
                        mm = pe.matmul(o[:, j * P:(j + 1) * P], av[:, c, hh:hh + 1].to_broadcast([P, P]), upper[:, :],
                                       start=True, stop=True)
                    close_bank(("acb", c, g), mm)
            o = open_bank("acb2")
            for hh in range(HEADS):
                mm = pe.matmul(o[0:T_S, hh * T_S:(hh + 1) * T_S], av[0:T_S, 2, hh:hh + 1].to_broadcast([T_S, T_S]),
                               upper_s[:, :], start=True, stop=True)
            close_bank("acb2", mm)
            pe.wait_ge(S["wmask"], 1)
            for q in range(2):
                o = open_bank(("wT", q))
                for j in range(4):
                    mm = pe.transpose(o[:, j * P:(j + 1) * P], wsp[:, 4 * q + j, :], ident[:, :])
                close_bank(("wT", q), mm)
            pe.wait_ge(S["bs_in"], 16)
            o = open_bank("bT")
            close_bank("bT", pe.transpose(o[:, 0:MHEADS], bsn[0:MHEADS, :], ident[0:MHEADS, 0:MHEADS]))
            for n in (("wT", 0), ("wT", 1), "bT"):
                stored(pe, n)
            o = open_bank("rep")
            pe.matmul(o[0:T_S, 0:32], rep4[:, :], wspT[0:L_S, :, 0:L_S], start=True, stop=True)
            mm = pe.matmul(o[0:T_S, 32:40], rep4[:, :], bsp[0:L_S, :], start=True, stop=True)
            close_bank("rep", mm)
            pe.wait_ge(S["xact_ok"], 8)
            for c in range(NCH):
                for n, k0, kn in (("xtm", 0, 4), ("btm", 4, 2)):
                    o = open_bank((n, c))
                    for j in range(kn):
                        mm = pe.transpose(o[0:ROWS[c], j * P:(j + 1) * P], xact[:, k0 + j, TOK[c]], ident[:, :])
                    close_bank((n, c), mm)
            for c in range(NCH):
                o = open_bank(("cb", c))
                for g in range(GROUPS):
                    mm = pe.matmul(o[0:ROWS[c], g * P:g * P + ROWS[c]], xact[:, 4 + g, TOK[c]], xact[:, 6 + g, TOK[c]],
                                   start=True, stop=True)
                close_bank(("cb", c), mm)
            for c in range(2):
                stored(pe, ("btm", c))
            pe.wait_ge(S["xdtd_ok"], 3)
            for c in range(2):
                o = open_bank(("st", c))
                for g in range(GROUPS):
                    mm = pe.matmul(o[:, 256 * g:256 * g + 256], btm[:, c, g, :], xdtd[:, c, 256 * g:256 * g + 256],
                                   start=True, stop=True)
                close_bank(("st", c), mm)

            def y_diag(c):
                stored(pe, ("cb", c))
                o = open_bank(("yd", c))
                for hh in range(HEADS):
                    lt = lmat[:, c, hh, :] if c < 2 else lmat_s[:, hh, :]
                    mm = pe.matmul(o[0:ROWS[c], hh * HD:(hh + 1) * HD], lt, xdt[0:ROWS[c], c, hh * HD:(hh + 1) * HD],
                                   start=True, stop=True)
                close_bank(("yd", c), mm)

            y_diag(0)
            y_diag(1)
            stored(pe, ("st", 0))
            o = open_bank("yo1")
            for g in range(GROUPS):
                mm = pe.matmul(o[:, 256 * g:256 * g + 256], xact[:, 6 + g, TOK[1]], hs1[:, 256 * g:256 * g + 256],
                               start=True, stop=True)
            close_bank("yo1", mm)
            y_diag(2)
            yos = [open_bank(("yos", g)) for g in range(GROUPS)]
            pe.wait_ge(S["h0_in"], 16)
            pe.wait_ge(S["cmask_ok"], 2)

            def h0_rows(b):
                o = open_bank(("h0T", b))
                for t in range(4):
                    mm = pe.transpose(o[:, t * P:(t + 1) * P], h0[:, b, t, :], ident[:, :])
                close_bank(("h0T", b), mm)

            h0_rows(0)
            for b in range(B_S):
                if b + 1 < B_S:
                    h0_rows(b + 1)
                stored(pe, ("h0T", b))
                for g in range(GROUPS):
                    mm = pe.matmul(yos[g][0:T_S, 0:256], cmask[:, g, b, :], h0t[:, b % 2, 256 * g:256 * g + 256],
                                   start=(b == 0), stop=(b == B_S - 1))
                    if b == B_S - 1:
                        close_bank(("yos", g), mm)
                    elif g == 1:
                        mm.then_inc(S["h0t_used"], 1)
            o = open_bank("decs")
            pe.wait_ge(S["aex_ok"], 1)
            for t in range(4):
                mm = pe.matmul(o[:, 8 * t:8 * t + 8], aex[0:T_S, t * P:(t + 1) * P], seq_s[:, :], start=True, stop=True)
            close_bank("decs", mm)
            stored(pe, ("st", 1))
            o = open_bank("hf")
            for t in range(4):
                mm = pe.transpose(o[:, t * P:(t + 1) * P], hs2[:, t * P:(t + 1) * P], ident[:, :])
            close_bank("hf", mm)
            stored(pe, "rep")
            for c in range(NCH):
                pe.wait_ge(S["vn_ok"], c + 1)
                o = open_bank(("sp", c))
                for hh in range(MHEADS):
                    lt = wspT[:, hh, :] if c < 2 else wsps[0:T_S, hh, :, :]
                    mm = pe.matmul(o[0:ROWS[c], hh * MHD:(hh + 1) * MHD], lt, vs[0:ROWS[c], c, hh * MHD:(hh + 1) * MHD],
                                   start=True, stop=True)
                close_bank(("sp", c), mm)
            for hf in range(2):
                for c in range(NCH):
                    pe.wait_ge(S["yn_ok" if hf == 0 else "m_ok"], (2 if hf == 0 else 1) * (c + 1))
                    src = (xs if hf == 0 else us)
                    o = open_bank(("cat", c, hf))
                    for j in range(4):
                        mm = pe.transpose(o[:, j * ROWS[c]:(j + 1) * ROWS[c]], src[0:ROWS[c], c, j * P:(j + 1) * P],
                                          ident[0:ROWS[c], 0:ROWS[c]])
                    close_bank(("cat", c, hf), mm)
            pe.wait_ge(S["bmask_ok"], 2)
            for t in range(4):
                for bh in range(2):
                    o = open_bank(("ns", t, bh))
                    mm = pe.matmul(o[:, :], xdtd[0:T_S, 2, t * P:(t + 1) * P],
                                   bmask[0:T_S, t // 2, 4 * bh:4 * bh + 4, :], start=True, stop=True)
                    close_bank(("ns", t, bh), mm)
            pe.wait_ge(S["wo_in"], 16)
            for ch in CH:
                stored(pe, ("cat", *ch))
            for c, hf in CH:
                o = open_bank(("wo", c, hf))
                for k in range(KD):
                    mm = pe.matmul(o[0:ROWS[c], :], aT[:, k, TOK[c]], w_o[:, k, 512 * hf:512 * hf + 512],
                                   start=(k == 0), stop=(k == KD - 1))
                close_bank(("wo", c, hf), mm)
            transposed("mT", mn, "mn_ok", CH)
            for ch in CH:
                stored(pe, ("mT", *ch))
            pe.wait_ge(S["wrt_in"], 16)
            o = open_bank("lg")
            for c in range(NCH):
                for k in range(KD):
                    mm = pe.matmul(o[0:ROWS[c], NE * c:NE * c + NE], aT[:, k, TOK[c]], wrt[:, k, :],
                                   start=(k == 0), stop=(k == KD - 1))
            close_bank("lg", mm)
            pe.wait_ge(S["mask_ok"], 3)
            o = open_bank("pos")
            pe.matmul(o[:, 0:NE], strict[:, :], msk[:, 0, 0:NE], start=True, stop=True)
            pe.matmul(o[:, NE:2 * NE], ones[:, :], msk[:, 0, 0:NE], start=True, stop=False)
            pe.matmul(o[:, NE:2 * NE], strict[:, :], msk[:, 1, 0:NE], start=False, stop=True)
            for c in range(2):
                pe.matmul(o[0:T_S, 2 * NE:3 * NE], ones[:, 0:T_S], msk[:, c, 0:NE], start=(c == 0), stop=False)
            pe.matmul(o[0:T_S, 2 * NE:3 * NE], strict[0:T_S, 0:T_S], msk[0:T_S, 2, 0:NE], start=False, stop=True)
            for c in range(NCH):
                mm = pe.matmul(o[0:1, 3 * NE:4 * NE], ones[0:ROWS[c], 0:1], msk[0:ROWS[c], c, 0:NE],
                               start=(c == 0), stop=(c == NCH - 1))
            close_bank("pos", mm)
            pe.wait_ge(S["gates_ok"], 3)
            o = open_bank("gT")
            for c in range(NCH):
                mm = pe.transpose(o[0:NE, TOK[c]], gat[0:ROWS[c], c, 0:NE], ident[0:ROWS[c], 0:ROWS[c]])
            close_bank("gT", mm)
            stored(pe, "gT")
            pe.wait_ge(S["bdn_in"], 16)
            for c, hf in CH:
                o = open_bank(("bd", c, hf))
                mm = pe.matmul(o[0:ROWS[c], :], gT[0:NE, TOK[c]], bdn[0:NE, 512 * hf:512 * hf + 512],
                               start=True, stop=True)
                close_bank(("bd", c, hf), mm)
            for b in range(8):
                pe.wait_ge(bank_free[b], BANK_END[1][b])

            def gather(x):
                for d in range(KD):
                    for c in range(NCH):
                        for t in range(3):
                            mm = pe.matmul(bank[2][:, CAP * d:CAP * d + CAP], mbf[:, c, t, d * P:(d + 1) * P],
                                           sel[:, x, c, :], start=(c == 0 and t == 0), stop=(c == 2 and t == 2))
                mm.then_inc(S["xt_full"], 1)

            pe.wait_ge(S["m3_ok"], 3)
            pe.wait_ge(S["sel_ok"], 1)
            gather(0)
            pe.wait_ge(S["npass_ok"], 1)
            for sem in (S["y_full"], *s_full):
                pe.sem_inc(sem, 1)
            n_pass = pe.value_load(npi[0:1, 0:1], min_val=1, max_val=PASSES)
            with pe.Fori(0, n_pass * (NE // 2)) as q:
                for x in range(2):
                    i = 2 * q + x
                    pe.wait_ge(S["up_free"], 2 * i + 1)
                    pe.wait_ge(S["bias_in"], 16 * i + 16)
                    for n in range(2):
                        for hf in range(2):
                            pe.matmul(bank[n][CAP * hf:CAP * hf + CAP, :], bias_ones[:, :],
                                      bias[:, 1024 * hf + 512 * n:1024 * hf + 512 * n + 512], start=True, stop=False)
                    pe.wait_ge(S["xt_ready"], i + 1)
                    for s in range(8):
                        pe.wait_ge(w_full[s], 16 * i + 16)
                        for n in range(2):
                            for hf in range(2):
                                mm = pe.matmul(bank[n][CAP * hf:CAP * hf + CAP, :], xT[:, x, s, :],
                                               slot(s)[:, 1024 * hf + 512 * n:1024 * hf + 512 * n + 512],
                                               start=False, stop=(s == 7))
                            if s == 7:
                                mm.then_inc(S["up_full"], 1)
                        if s < 7:
                            mm.then_inc(S["w_used"], 1)
                    pe.wait_ge(S["sel_ok"], i + 2)
                    gather(1 - x)
                    if x == 1:
                        pe.wait_ge(S["g_ok"], i + 1)
                        pe.wait_ge(S["at_free"], 3 * q + 2)
                        for c in range(NCH):
                            mm = pe.transpose(bank[3][:, TOK[c]], gsel[0:ROWS[c], c, :], ident[0:ROWS[c], 0:ROWS[c]])
                        mm.then_inc(S["at_full"], 1)
                    pe.wait_ge(S["at_free"], 3 * q + 2 * x + 1)
                    for f in range(4):
                        if f % 2 == 0:
                            pe.wait_ge(S["act_ready"], 2 * i + 2 + f // 2)
                        mm = pe.transpose(bank[3][:, f * P:(f + 1) * P], act_h[:, f * P:(f + 1) * P], ident[:, :])
                    mm.then_inc(S["at_full"], 1)
                    pe.wait_ge(S["ysb_ok"], 2 * i + 1)
                    pe.wait_ge(S["at_free"], 3 * q + 2 * x + 2)
                    for k in range(8):
                        if k % 2 == 0:
                            pe.wait_ge(w_full[8 + k // 2], 16 * i + 16)
                        for hf in range(2):
                            mm = pe.matmul(bank[4][CAP * hf:CAP * hf + CAP, :], actT[:, k % 4, k // 4, :],
                                           slot(8 + k // 2)[:, 1024 * (k % 2) + 512 * hf:1024 * (k % 2) + 512 * hf + 512],
                                           start=(k == 0), stop=(k == 7))
                        if k == 7:
                            mm.then_inc(S["y_full"], 1)
                        elif k % 2:
                            mm.then_inc(S["w_used"], 1)
                pe.wait_ge(S["ysb_ok"], 4 * q + 5)
                for j, (c, hf) in enumerate(CH):
                    pe.wait_ge(s_free[j % 3], 2 * q + j // 3 + 1)
                    pe.matmul(bank[5 + j % 3][0:ROWS[c], :], gselT[:, TOK[c]], ysb[:, 512 * hf:512 * hf + 512],
                              start=True, stop=True).then_inc(s_full[j % 3], 1)

            pe.wait_ge(S["moe_done"], 1)
            pe.wait_ge(S["pr_in"], 32)
            for k in range(2):
                o = open_bank(("pT", k))
                for c in range(NCH):
                    mm = pe.transpose(o[:, TOK[c]], prows[0:ROWS[c], c, k * P:(k + 1) * P], ident[0:ROWS[c], 0:ROWS[c]])
                close_bank(("pT", k), mm)
            pe.wait_ge(S["pw_in"], 48)
            for k in range(2):
                stored(pe, ("pT", k))
            for c, hf in CH:
                o = open_bank(("pp", c, hf))
                for k in range(2):
                    mm = pe.matmul(o[0:ROWS[c], :], pT[:, k, TOK[c]], w_pp[:, k, 512 * hf:512 * hf + 512],
                                   start=(k == 0), stop=(k == 1))
                close_bank(("pp", c, hf), mm)
            transposed("nT", hn, "hn_ok", CH)
            for c, hf in CH:
                if hf == 0:
                    stored(pe, ("nT", c, 0))
                    stored(pe, ("nT", c, 1))
                o = open_bank(("pg", c, hf))
                for k in range(KD):
                    mm = pe.matmul(o[0:ROWS[c], :], aT[:, k, TOK[c]], w_pg[:, k, 512 * hf:512 * hf + 512],
                                   start=(k == 0), stop=(k == KD - 1))
                close_bank(("pg", c, hf), mm)

        @block.scalar
        def _(act):
            n_done = [0]

            def step(ins):
                n_done[0] += 1
                ins.then_inc(S["ach"], 1)
                act.wait_ge(S["ach"], n_done[0])

            act.dma_start(prow[0:24, :], I["state_conv"][0].rearrange("b k n -> (b k) n")).then_inc(S["par_in"], 16)
            act.dma_start(prow[24:28, :], I["conv_w"][0]).then_inc(S["par_in"], 16)
            act.dma_start(prow[28:29, :], I["conv_b"]).then_inc(S["par_in"], 16)
            act.dma_start(prow[29:30, :], I["norm_mix_g"]).then_inc(S["par_in"], 16)
            act.dma_start(prow[30:31, 0:SSD], I["ssd_norm_g"]).then_inc(S["par_in"], 16)
            act.dma_start(prow[30:31, SSD:D], I["mlp_out_g"]).then_inc(S["par_in"], 16)
            act.dma_start(prow[31:32, :], I["norm_moe_g"]).then_inc(S["par_in"], 16)
            act.dma_start(prow[32:33, :], I["norm_ple_g"]).then_inc(S["par_in"], 16)
            act.dma_start(wsp, I["w_spatial"][0].rearrange("h i j -> i h j")).then_inc(S["wsp_in"], 16)
            act.dma_start(bsn[0:MHEADS, :], I["b_spatial"][0]).then_inc(S["bs_in"], 16)
            act.dma_start(vgb[:, 0, :], I["v_norm_g"][0].partition_broadcast(P)).then_inc(S["vgb_in"], 16)
            act.dma_start(vgb[:, 1, :], I["v_norm_b"][0].partition_broadcast(P)).then_inc(S["vgb_in"], 16)
            act.dma_start(bup_f, I["b_up"][0].rearrange("e (q n) -> (e q) n", n=512)).then_inc(S["bup_in"], 16)
            act.dma_start(wrt, I["w_router"][0].rearrange("(k p) n -> p k n", p=P)).then_inc(S["wrt_in"], 16)
            act.dma_start(brow[:, :], I["b_router"][0].partition_broadcast(P)).then_inc(S["brow_in"], 16)

            def rstd(out, sums, n, total, wait, count):
                act.wait_ge(S[wait], count)
                step(act.activation(out, sums, ACT.Ln, scale=1.0 / total, bias=eps[:, 0:1]))
                act.activation(out, out, ACT.Exp, scale=-0.5).then_inc(S[n], 1)

            act.wait_ge(S["vinit"], 1)
            act.wait_ge(S["x_in"], 48)
            for c in range(NCH):
                r = slice(0, ROWS[c])
                if c:
                    act.wait_ge(S["sumsq"], c)
                act.activation(junk_x[r, :], h[r, c, :], ACT.Square, accum_out=ss_x[r, c:c + 1]).then_inc(S["sumsq"], 1)
            rstd(rs_x, ss_x, "rstd_x", D, "sumsq", 3)

            o = filled(act, "par")
            act.wait_ge(freed("par"), 1)
            act.activation(xps[:, :, 0:3, :],
                           o[:, 0:33 * KD].rearrange("p (k n) -> p k n", k=KD)[:, :, 0:24]
                           .rearrange("p k (b j) -> p k j b", b=B_S), ACT.Copy).then_inc(freed("par"), 1)
            for t in range(8):
                o = filled(act, ("xbc", t))
                act.activation(xp[:, t, 3:T_PROMPT + 3], o[:, 0:T_PROMPT], ACT.Copy).then_inc(freed(("xbc", t)), 1)
                act.activation(xps[:, t, 3:, :], o[:, T_PROMPT:T].rearrange("p (b s) -> p s b", b=B_S), ACT.Copy)\
                   .then_inc(freed(("xbc", t)), 1)
            act.wait_ge(S["bup_stored"], 16)
            for n, dst in (("cvp", cvp), ("cvs", cvs)):
                for hf in range(2):
                    o = filled(act, (n, hf))
                    act.activation(dst[0:T_S, 512 * hf:512 * hf + 512], o[0:T_S, :], ACT.Copy).then_inc(freed((n, hf)), 1)
            for t in range(8):
                act.wait_ge(S["conv_ok"], 2 * t + 2)
                act.activation(xact[:, t, :], xact[:, t, :], ACT.Silu).then_inc(S["xact_ok"], 1)
            for c in range(NCH):
                r = slice(0, ROWS[c])
                o = filled(act, ("z", c))
                act.activation(zs[r, c, :], o[r, :], ACT.Silu).then_inc(freed(("z", c)), 1)
            for n, dst in (("u", us), ("v", vs)):
                for c in range(NCH):
                    r = slice(0, ROWS[c])
                    o = filled(act, (n, c))
                    act.activation(dst[r, c, :], o[r, :], ACT.Gelu_apprx_tanh).then_inc(freed((n, c)), 1)
            act.wait_ge(S["dtabs"], 1)
            act.activation(dtb, dta, ACT.Exp, scale=-1.0).then_inc(S["dtexp"], 1)
            act.wait_ge(S["dtadd"], 1)
            act.activation(av, dtc, ACT.Ln).then_inc(S["dtln"], 1)
            act.wait_ge(S["pb_in"], 48)
            act.activation(aneg, pb[:, HEADS:2 * HEADS], ACT.Exp).then_inc(S["anexp"], 1)
            act.wait_ge(S["dec_in"], 1)
            act.activation(eac, acum, ACT.Exp).then_inc(S["eac_ok"], 1)
            act.activation(dec, dec, ACT.Exp).then_inc(S["eac_ok"], 1)
            act.activation(edec, atot[:, 1, :], ACT.Exp).then_inc(S["eac_ok"], 1)
            for c in range(2):
                for g in range(GROUPS):
                    stored(act, ("acb", c, g))
                    act.activation(lmat[:, c, 4 * g:4 * g + 4, :], lmat[:, c, 4 * g:4 * g + 4, :], ACT.Exp)\
                       .then_inc(S["lexp"], 1)
            stored(act, "acb2")
            act.activation(lmat_s, lmat_s, ACT.Exp).then_inc(S["lexp"], 1)
            for q in range(2):
                o = filled(act, ("wT", q))
                act.activation(wspT[:, 4 * q:4 * q + 4, :].rearrange("p h i -> p (h i)"), o[:, :], ACT.Copy)\
                   .then_inc(freed(("wT", q)), 1)
            rstd(rs_v, mv[:, :, 1], "rsv", 1, "rsv_in", 1)
            for c in range(NCH):
                r = slice(0, ROWS[c])
                o = filled(act, ("xtm", c))
                act.activation(xs[r, c, :], o[r, :], ACT.Copy).then_inc(freed(("xtm", c)), 1)
                o = filled(act, ("btm", c))
                act.activation(btm[r, c, :, :].rearrange("p g n -> p (g n)"), o[r, 0:256], ACT.Copy)\
                   .then_inc(freed(("btm", c)), 1)
            for b in range(B_S):
                if b >= 2:
                    act.wait_ge(S["h0t_used"], b - 1)
                o = filled(act, ("h0T", b))
                act.activation(h0t[:, b % 2, :], o[:, :], ACT.Copy).then_inc(freed(("h0T", b)), 1)
            o = filled(act, "decs")
            act.activation(decs[:, :, :].rearrange("p t b -> p (t b)"), o[:, 0:32], ACT.Exp).then_inc(freed("decs"), 1)
            o = filled(act, "hf")
            act.activation(xdt[:, 0, :], o[:, :], ACT.Copy).then_inc(freed("hf"), 1)
            for c in range(NCH):
                r = slice(0, ROWS[c])
                act.wait_ge(S["y_ok"], c + 1)
                for g in range(GROUPS):
                    if c or g:
                        act.wait_ge(S["ygs"], 2 * c + g)
                    act.activation(junk[r, 0:256], xs[r, c, 256 * g:256 * g + 256], ACT.Square,
                                   accum_out=ss_g[r, 2 * c + g:2 * c + g + 1]).then_inc(S["ygs"], 1)
            rstd(rs_g, ss_g, "rs_g_ok", 256, "ygs", 6)
            for c in range(NCH):
                r = slice(0, ROWS[c])
                act.wait_ge(S["mix_ok"], c + 1)
                if c:
                    act.wait_ge(S["mss"], c)
                act.activation(junk[r, :], us[r, c, :], ACT.Square, accum_out=ss_m[r, c:c + 1]).then_inc(S["mss"], 1)
            rstd(rs_m, ss_m, "rs_m_ok", MLP, "mss", 3)
            jh = view(0, D)
            for c in range(NCH):
                r = slice(0, ROWS[c])
                stored(act, ("wo", c, 0))
                stored(act, ("wo", c, 1))
                if c:
                    act.wait_ge(S["hss"], c)
                act.activation(jh[r, :], h[r, c, :], ACT.Square, accum_out=ss_o[r, c:c + 1]).then_inc(S["hss"], 1)
            rstd(rs_o, ss_o, "rs_o_ok", D, "hss", 3)
            act.wait_ge(S["mbf_zero"], 1)
            for c in range(NCH):
                r = slice(0, ROWS[c])
                act.wait_ge(S["mn_ok"], c + 1)
                act.activation(mbf[r, c, 0, :], mn[r, c, :], ACT.Copy).then_inc(S["m1_ok"], 1)
            for c in range(NCH):
                r = slice(0, ROWS[c])
                act.wait_ge(S["r1_ok"], c + 1)
                act.activation(mbf[r, c, 1, :], mr[r, c, :], ACT.Copy).then_inc(S["m2_ok"], 1)
            for c in range(NCH):
                r = slice(0, ROWS[c])
                act.wait_ge(S["ngm_ok"], c + 1)
                act.activation(ex[r, c, 0:NE], lgt[r, c, 0:NE], ACT.Exp, bias=top4[r, c, 7:8]).then_inc(S["gex"], 1)
            o = filled(act, "gT")
            act.activation(gT[0:NE, :], o[0:NE, 0:T], ACT.Copy).then_inc(freed("gT"), 1)
            act.wait_ge(S["npass_ok"], 1)
            for sem in (S["at_free"], S["ysb_ok"]):
                act.sem_inc(sem, 1)
            n_pass = act.value_load(npi[0:1, 0:1], min_val=1, max_val=PASSES)
            with act.Fori(0, n_pass * (NE // 2)) as q:
                for x in range(2):
                    i = 2 * q + x
                    act.wait_ge(S["act_ready"], 2 * i + 1)
                    for n in range(2):
                        act.wait_ge(S["g_ready"], 2 * i + 1 + n)
                        act.activation(sq[:, 256 * n:256 * n + 256], sg[:, 256 * n:256 * n + 256], ACT.Sigmoid,
                                       scale=ALPHA).then_inc(S["sig_ready"], 1)
                    act.wait_ge(s_full[2], 2 * q + 1)
                    if x == 1:
                        act.wait_ge(S["at_full"], 3 * q + 2)
                        act.activation(gselT, bank[3][:, 0:T], ACT.Copy).then_inc(S["at_free"], 1)
                    act.wait_ge(S["y_full"], i + 1)
                    act.wait_ge(S["at_full"], 3 * q + 2 * x + 1)
                    act.activation(actT.rearrange("p f a s -> p (f a s)"), bank[3][:, :], ACT.Copy)\
                       .then_inc(S["at_free"], 1)
                    act.wait_ge(S["y_full"], i + 2)
                    act.activation(ysb[CAP * x:CAP * x + CAP, 0:512], bank[4][0:CAP, :], ACT.Copy)\
                       .then_inc(S["ysb_ok"], 1)
            act.wait_ge(S["moe_done"], 1)
            jt = view(13408, D)
            for c in range(NCH):
                r = slice(0, ROWS[c])
                if c:
                    act.wait_ge(S["fss"], c)
                act.activation(jt[r, :], h[r, c, :], ACT.Square, accum_out=ss_p[r, c:c + 1]).then_inc(S["fss"], 1)
            rstd(rs_p, ss_p, "rs_p_ok", D, "fss", 3)
            for c in range(NCH):
                for hf in range(2):
                    r = slice(0, ROWS[c])
                    o = filled(act, ("pp", c, hf))
                    act.activation(pp[r, c, 512 * hf:512 * hf + 512], o[r, :], ACT.Copy).then_inc(freed(("pp", c, hf)), 1)
            for c in range(NCH):
                for hf in range(2):
                    r = slice(0, ROWS[c])
                    o = filled(act, ("pg", c, hf))
                    act.activation(pgs[r, c, 512 * hf:512 * hf + 512], o[r, :], ACT.Sigmoid).then_inc(freed(("pg", c, hf)), 1)
            for c in range(NCH):
                r = slice(0, ROWS[c])
                act.wait_ge(S["hfin"], c + 1)
                if c:
                    act.wait_ge(S["fin_ss"], c)
                act.activation(jt[r, :], h[r, c, :], ACT.Square, accum_out=ss_f[r, c:c + 1]).then_inc(S["fin_ss"], 1)
            rstd(rs_f, ss_f, "rs_f_ok", D, "fin_ss", 3)

        @block.vector
        def _(dve):
            n_done = [0]

            def put(ins):
                n_done[0] += 1
                ins.then_inc(S["vch"], 1)
                return n_done[0]

            def after(n):
                dve.wait_ge(S["vch"], n)

            def step(ins):
                after(put(ins))

            tt, ts, stt = dve.tensor_tensor, dve.tensor_scalar, dve.scalar_tensor_tensor
            step(dve.memset(stat[:, :, :], 0.0))
            step(dve.memset(gstat[:, :, :], 0.0))
            step(dve.memset(mv[:, :, :], 0.0))
            step(dve.memset(small[:, :, :], 0.0))
            dve.memset(eps[:, :], EPS).then_inc(S["vinit"], 1)

            dve.wait_ge(S["rstd_x"], 1)
            for c in range(NCH):
                r = slice(0, ROWS[c])
                ts(xn[r, c, :], h[r, c, :], rs_x[r, c:c + 1], None, ALU.mult).then_inc(S["xn_ok"], 1)
            o = filled(dve, "par")
            dve.tensor_copy(pf[:, :, :], o[:, 0:33 * KD].rearrange("p (k n) -> p k n", k=KD)[:, :, 24:33])\
               .then_inc(freed("par"), 1)
            stored(dve, "par")

            def turned(tag, g, order):
                for c, hf in order:
                    o = filled(dve, (tag, c, hf))
                    n = ROWS[c]
                    tt(aT[:, 4 * hf:4 * hf + 4, TOK[c]], o[:, 0:4 * n].rearrange("p (k t) -> p k t", k=4),
                       over(pf[:, 4 * hf:4 * hf + 4, g], [P, 4, n]), ALU.mult).then_inc(freed((tag, c, hf)), 1)

            turned("xT", 5, CH)
            dve.wait_ge(S["pb_in"], 48)
            o = filled(dve, "dt")
            for c in range(NCH):
                r = slice(0, ROWS[c])
                tt(dtr[r, c, :], o[r, 8 * c:8 * c + 8], pb[r, 0:HEADS], ALU.add).then_inc(freed("dt"), 1)
            stored(dve, "dt")
            stt(dta, dtr, -1.0, dtr, ALU.mult, ALU.max).then_inc(S["dtabs"], 1)
            dve.wait_ge(S["pads"], 1)
            for t in range(8):
                stored(dve, ("xbc", t))
                outs = (xact[:, t, 0:T_PROMPT], xact[:, t, T_PROMPT:].rearrange("p (b s) -> p s b", b=B_S))

                def tap(n, j):
                    return xp[:, t, j:j + T_PROMPT] if n == 0 else xps[:, t, j:j + L_S, :]

                last = [put(ts(outs[n], tap(n, 0), pf[:, t, 0:1], pf[:, t, 4:5], ALU.mult, ALU.add)) for n in range(2)]
                for j in range(1, 4):
                    for n in range(2):
                        after(last[n])
                        ins = stt(outs[n], tap(n, j), pf[:, t, j:j + 1], outs[n], ALU.mult, ALU.add)
                        if j == 3:
                            ins.then_inc(S["conv_ok"], 1)
                        else:
                            last[n] = put(ins)
            dve.wait_ge(S["dtexp"], 1)
            ts(dtc, dtb, 1.0, None, ALU.add).then_inc(S["dtadd"], 1)
            dve.wait_ge(S["dtadd"], 1)
            step(ts(dta, dtc, -1.0, None, ALU.add))
            dve.wait_ge(S["dtln"], 1)
            step(ts(dtc, dta, 0.0, None, ALU.is_equal))
            step(tt(dta, dta, dtc, ALU.add))
            step(tt(av, av, dtc, ALU.add))
            step(dve.reciprocal(dta, dta))
            step(tt(dta, dta, av, ALU.mult))
            step(tt(dta, dta, dtb, ALU.mult))
            step(stt(dt, dtr, 0.0, dta, ALU.max, ALU.add))
            dve.wait_ge(S["anexp"], 1)
            stt(av, dt, -1.0, aneg.unsqueeze(1).to_broadcast([P, NCH, HEADS]), ALU.mult, ALU.mult).then_inc(S["a_ok"], 1)
            dve.wait_ge(S["a_ok"], 1)
            for c in range(NCH):
                r = slice(0, ROWS[c])
                stored(dve, ("v", c))
                n = put(dve.bn_stats(bn[r, c, :], vs[r, c, :]))
            after(n)
            for c in range(NCH):
                r = slice(0, ROWS[c])
                n = put(dve.bn_aggr(mv[r, c, :], bn[r, c, :]))
            after(n)
            step(dve.memset(npf[0:1, 6:7], 0.0))
            dve.memset(npf[0:1, 7:8], 0.0).then_inc(S["rsv_in"], 1)
            dve.wait_ge(S["bup_stored"], 16)
            dve.tensor_copy(hs3(aex[0:T_S, :]), over(av[0:T_S, 2, :], [T_S, HEADS, HD])).then_inc(S["aex_ok"], 1)
            o = filled(dve, "acum")
            dve.tensor_copy(acum[:, 0:2, :].rearrange("p c h -> p (c h)"), o[:, 0:16]).then_inc(freed("acum"), 1)
            dve.tensor_copy(small[0:T_S, 6:8, 16:24], o[0:T_S, 16:32].rearrange("p (a h) -> p a h", a=2))\
               .then_inc(freed("acum"), 1)
            stored(dve, "acum")
            for c in range(2):
                for g in range(GROUPS):
                    o = filled(dve, ("acb", c, g))
                    rows = o[:, :].rearrange("p (h i) -> p h i", h=HPG)
                    dve.tensor_copy(atot[:, c, 4 * g:4 * g + 4], rows[:, :, P - 1]).then_inc(freed(("acb", c, g)), 1)
                    for j in range(HPG):
                        hh = HPG * g + j
                        stt(lmat[:, c, hh, :], rows[:, j, :], acum[:, c, hh:hh + 1], negm[:, :],
                            ALU.subtract, ALU.add).then_inc(freed(("acb", c, g)), 1)
            o = filled(dve, "acb2")
            for hh in range(HEADS):
                stt(lmat_s[:, hh, :], o[0:T_S, hh * T_S:(hh + 1) * T_S], acum[0:T_S, 2, hh:hh + 1], negm_s[:, :],
                    ALU.subtract, ALU.add).then_inc(freed("acb2"), 1)
            for c in range(2):
                for g in range(GROUPS):
                    stored(dve, ("acb", c, g))
            tt(dec, atot, acum, ALU.subtract).then_inc(S["dec_in"], 1)
            o = filled(dve, "bT")
            dve.tensor_copy(bsp[:, :], o[:, 0:MHEADS]).then_inc(freed("bT"), 1)
            o = filled(dve, "rep")
            for_b = o[0:T_S, 0:32].rearrange("p (h i) -> p h i", h=MHEADS).unsqueeze(2).to_broadcast([T_S, MHEADS, B_S, L_S])
            tt(wsps[0:T_S, :, :, :], for_b, block_s[:, :].rearrange("p (b s) -> p b s", b=B_S).unsqueeze(1)
               .to_broadcast([T_S, MHEADS, B_S, L_S]), ALU.mult).then_inc(freed("rep"), 1)
            dve.tensor_copy(bss[:, :], o[0:T_S, 32:40]).then_inc(freed("rep"), 1)
            dve.wait_ge(S["rsv"], 1)
            dve.wait_ge(S["vgb_in"], 32)
            for c in range(NCH):
                r = slice(0, ROWS[c])
                n = put(ts(vs[r, c, :], vs[r, c, :], mv[r, c, 0:1], rs_v[r, c:c + 1], ALU.subtract, ALU.mult))
            after(n)
            for c in range(NCH):
                r = slice(0, ROWS[c])
                n = put(tt(vs[r, c, :], vs[r, c, :], vgb[r, 0, :], ALU.mult))
            after(n)
            for c in range(NCH):
                r = slice(0, ROWS[c])
                tt(vs[r, c, :], vs[r, c, :], vgb[r, 1, :], ALU.add).then_inc(S["vn_ok"], 1)
            dve.wait_ge(S["eac_ok"], 3)
            dve.wait_ge(S["cv_out"], 16 * L_S)
            for c in range(NCH):
                r, n = slice(0, ROWS[c]), ROWS[c]
                stored(dve, ("xtm", c))
                step(tt(hs3(xdt[r, c, :]), hs3(xs[r, c, :]), over(dt[r, c, :], [n, HEADS, HD]), ALU.mult))
                tt(hs3(xdtd[r, c, :]), hs3(xdt[r, c, :]), over(dec[r, c, :], [n, HEADS, HD]), ALU.mult)\
                    .then_inc(S["xdtd_ok"], 1)
                n_skip = put(tt(hs3(xs[r, c, :]), hs3(xs[r, c, :]), over(pb[r, 16:24], [n, HEADS, HD]), ALU.mult))
            dve.wait_ge(S["lexp"], 5)
            for c in range(NCH):
                o = filled(dve, ("cb", c))
                for g in range(GROUPS):
                    n = ROWS[c]
                    part = lmat[:, c, 4 * g:4 * g + 4, :] if c < 2 else lmat_s[:, 4 * g:4 * g + 4, :]
                    tt(part, part, o[0:n, g * P:g * P + n].unsqueeze(1).to_broadcast([n, HPG, n]), ALU.mult)\
                        .then_inc(freed(("cb", c)), 1)
            stored(dve, ("wT", 1))
            o = filled(dve, ("st", 0))
            dve.tensor_copy(hs1, o[:, :]).then_inc(freed(("st", 0)), 1)
            stored(dve, ("st", 0))
            step(tt(hs3(hs2), hs3(hs1), over(edec, [P, HEADS, HD]), ALU.mult))
            o = filled(dve, ("st", 1))
            tt(hs2, hs2, o[:, :], ALU.add).then_inc(freed(("st", 1)), 1)
            for g in range(GROUPS):
                tt(cmask[:, g, :, :], xact[:, 6 + g, T_PROMPT:].unsqueeze(1).to_broadcast([P, B_S, T_S]), seqm, ALU.mult)\
                    .then_inc(S["cmask_ok"], 1)
            stored(dve, ("btm", 2))
            for g in range(GROUPS):
                tt(bmask[0:T_S, g, :, :], btm[0:T_S, 2, g, :].unsqueeze(1).to_broadcast([T_S, B_S, N_ST]),
                   over(seq_s[:, :], [T_S, B_S, N_ST]), ALU.mult).then_inc(S["bmask_ok"], 1)
            after(n_skip)
            yoff = view(21248, 512)
            for c in (0, 1, 2):
                r, n = slice(0, ROWS[c]), ROWS[c]
                o = filled(dve, ("yd", c))
                tt(xs[r, c, :], xs[r, c, :], o[r, :], ALU.add).then_inc(freed(("yd", c)), 1)
                stored(dve, ("yd", c))
                if c == 1:
                    o = filled(dve, "yo1")
                    tt(hs3(yoff), hs3(o[:, :]), over(eac[:, 1, :], [P, HEADS, HD]), ALU.mult).then_inc(freed("yo1"), 1)
                    stored(dve, "yo1")
                if c == 2:
                    for g in range(GROUPS):
                        o = filled(dve, ("yos", g))
                        tt(hs3(yoff[0:T_S, 256 * g:256 * g + 256]), hs3(o[0:T_S, 0:256]),
                           over(eac[0:T_S, 2, 4 * g:4 * g + 4], [T_S, HPG, HD]), ALU.mult).then_inc(freed(("yos", g)), 1)
                        stored(dve, ("yos", g))
                if c:
                    step(tt(xs[r, c, :], xs[r, c, :], yoff[r, :], ALU.add))
                tt(xs[r, c, :], xs[r, c, :], zs[r, c, :], ALU.mult).then_inc(S["y_ok"], 1)
            for c in range(NCH):
                r, n = slice(0, ROWS[c]), ROWS[c]
                bs = bsp[:, :] if c < 2 else bss[:, :]
                o = filled(dve, ("sp", c))
                dve.wait_ge(S["y_ok"], c + 1)
                tt(hs3(zs[r, c, :]), hs3(o[r, :]), over(bs, [n, MHEADS, MHD]), ALU.add).then_inc(freed(("sp", c)), 1)
                stored(dve, ("sp", c))
                tt(us[r, c, :], us[r, c, :], zs[r, c, :], ALU.mult).then_inc(S["mix_ok"], 1)
            dve.wait_ge(S["rs_g_ok"], 1)
            for c in range(NCH):
                r = slice(0, ROWS[c])
                for g in range(GROUPS):
                    ts(xs[r, c, 256 * g:256 * g + 256], xs[r, c, 256 * g:256 * g + 256],
                       rs_g[r, 2 * c + g:2 * c + g + 1], None, ALU.mult).then_inc(S["yn_ok"], 1)
            turned("cat", 6, [(c, 0) for c in range(NCH)])
            dve.wait_ge(S["rs_m_ok"], 1)
            for c in range(NCH):
                r = slice(0, ROWS[c])
                ts(us[r, c, :], us[r, c, :], rs_m[r, c:c + 1], None, ALU.mult).then_inc(S["m_ok"], 1)
            turned("cat", 6, [(c, 1) for c in range(NCH)])
            dve.wait_ge(S["h0_in"], 16)
            stored(dve, "decs")
            for t in range(4):
                for bh in range(2):
                    o = filled(dve, ("ns", t, bh))
                    for j in range(4):
                        b = 4 * bh + j
                        stt(h0[:, b, t, :], h0[:, b, t, :], decs[:, t, b:b + 1], o[:, j * P:(j + 1) * P],
                            ALU.mult, ALU.add).then_inc(freed(("ns", t, bh)), 1)
            for c in range(NCH):
                for hf in range(2):
                    r = slice(0, ROWS[c])
                    o = filled(dve, ("wo", c, hf))
                    part = h[r, c, 512 * hf:512 * hf + 512]
                    tt(part, part, o[r, :], ALU.add).then_inc(freed(("wo", c, hf)), 1)
            dve.wait_ge(S["rs_o_ok"], 1)
            dve.wait_ge(S["v_out"], 16)
            dve.wait_ge(S["hf_out"], 16)
            for c in range(NCH):
                r = slice(0, ROWS[c])
                ts(mn[r, c, :], h[r, c, :], rs_o[r, c:c + 1], None, ALU.mult).then_inc(S["mn_ok"], 1)
            dve.memset(mbf[:, 2, :, :], 0.0).then_inc(S["mbf_zero"], 1)
            dve.memset(bias, 0.0).then_inc(S["bias_zero"], 1)
            dve.memset(bdn[0:1, 0:1], 0.0).then_inc(S["mix_done"], 1)
            step(dve.memset(bias_ones[:, :], 0.0))
            step(dve.memset(bias_ones[0:3, :], 1.0))
            step(dve.memset(lgt, BIG))
            step(dve.memset(top4, BIG))
            step(dve.memset(gat, 0.0))
            step(dve.memset(prk, 0.0))
            step(dve.memset(gsel, 0.0))
            step(dve.memset(pos_t, -1.0))
            step(dve.memset(gate_t, 0.0))
            turned("mT", 7, CH)
            for c in range(NCH):
                r = slice(0, ROWS[c])
                dve.wait_ge(S["m1_ok"], c + 1)
                tt(mr[r, c, :], mn[r, c, :], mbf[r, c, 0, :], ALU.subtract).then_inc(S["r1_ok"], 1)
            dve.wait_ge(S["brow_in"], 16)
            o = filled(dve, "lg")
            for c in range(NCH):
                r = slice(0, ROWS[c])
                tt(lgt[r, c, 0:NE], o[r, NE * c:NE * c + NE], brow[r, :], ALU.add).then_inc(freed("lg"), 1)
            stored(dve, "lg")
            for c in range(NCH):
                r = slice(0, ROWS[c])
                step(dve.max(top8[r, c, :], lgt[r, c, 0:NE]))
                step(dve.tensor_copy(top4[r, c, 0:4], top8[r, c, 0:4]))
                step(dve.match_replace(mrep[r, c, :], top4[r, c, :], lgt[r, c, :], -BIG))
                tt(msk[r, c, 0:NE], mrep[r, c, 0:NE], lgt[r, c, 0:NE], ALU.not_equal).then_inc(S["mask_ok"], 1)
                ts(top4[r, c, 7:8], top8[r, c, 0:1], -1.0, None, ALU.mult).then_inc(S["ngm_ok"], 1)
            dve.wait_ge(S["mask_ok"], 3)
            for c in range(NCH):
                r = slice(0, ROWS[c])
                dve.wait_ge(S["gex"], c + 1)
                step(dve.tensor_tensor_reduce(gat[r, c, 0:NE], ex[r, c, 0:NE], msk[r, c, 0:NE], 1.0, 0.0,
                                              ALU.mult, ALU.add, gsum[r, c:c + 1]))
                step(dve.reciprocal(grec[r, c:c + 1], gsum[r, c:c + 1]))
                ts(gat[r, c, 0:NE], gat[r, c, 0:NE], grec[r, c:c + 1], None, ALU.mult).then_inc(S["gates_ok"], 1)
            o = filled(dve, "pos")
            for c in range(NCH):
                r = slice(0, ROWS[c])
                stt(prk[r, c, 0:NE], o[r, NE * c:NE * c + NE], 1.0, msk[r, c, 0:NE], ALU.add, ALU.mult)\
                    .then_inc(freed("pos"), 1)
            dve.tensor_reduce(npf[0:1, 0:1], o[0:1, 3 * NE:4 * NE], AX_X, ALU.max).then_inc(freed("pos"), 1)
            stored(dve, "pos")
            step(ts(npf[0:1, 1:PASSES], thr[:, :], npf[0:1, 0:1], None, ALU.is_lt))
            step(dve.tensor_reduce(npf[0:1, 5:6], npf[0:1, 1:PASSES], AX_X, ALU.add))
            step(ts(npf[0:1, 6:7], npf[0:1, 5:6], 1.0, None, ALU.add))
            dve.tensor_copy(npi[:, :], npf[0:1, 6:7]).then_inc(S["npass_ok"], 1)
            dve.wait_ge(S["gates_ok"], 3)
            for p in range(PASSES):
                n = put(ts(pos_t[:, :, NE * p:NE * p + NE], prk[:, :, 0:NE], float(-1 - CAP * p), None, ALU.add))
                n = put(dve.tensor_copy(gate_t[:, :, NE * p:NE * p + NE], gat[:, :, 0:NE]))
            after(n)

            def pick(x, i):
                at = pos_t[:, :, bass.ds(i, 1)].to_broadcast([P, NCH, CAP])
                tt(sel[:, x, :, :], iota[:, :].unsqueeze(1).to_broadcast([P, NCH, CAP]), at, ALU.is_equal)\
                    .then_inc(S["sel_ok"], 1)

            pick(0, 0)
            for c in range(NCH):
                r = slice(0, ROWS[c])
                dve.wait_ge(S["m2_ok"], c + 1)
                tt(mbf[r, c, 2, :], mr[r, c, :], mbf[r, c, 1, :], ALU.subtract).then_inc(S["m3_ok"], 1)
            dve.wait_ge(S["m3_ok"], NCH)
            for c in range(NCH):
                for hf in range(2):
                    r = slice(0, ROWS[c])
                    o = filled(dve, ("bd", c, hf))
                    part = h[r, c, 512 * hf:512 * hf + 512]
                    tt(part, part, o[r, :], ALU.add).then_inc(freed(("bd", c, hf)), 1)
            for ch in CH:
                stored(dve, ("bd", *ch))

            def gathered(x, n):
                dve.wait_ge(S["xt_full"], n)
                tt(xT[:, x, :, :], bank[2][:, :].rearrange("p (k s) -> p k s", k=KD), over(pf[:, :, 7], [P, KD, CAP]),
                   ALU.mult).then_inc(S["xt_ready"], 1)

            gathered(0, 1)
            dve.wait_ge(S["npass_ok"], 1)
            for sem in (S["up_free"], S["act_ready"], *s_free):
                dve.sem_inc(sem, 1)
            n_pass = dve.value_load(npi[0:1, 0:1], min_val=1, max_val=PASSES)
            with dve.Fori(0, n_pass * (NE // 2)) as q:
                for x in range(2):
                    i = 2 * q + x
                    pick(1 - x, i + 1)
                    dve.wait_ge(S["sel_ok"], i + 1)
                    tt(gsel[:, :, CAP * x:CAP * x + CAP], sel[:, x, :, :],
                       gate_t[:, :, bass.ds(i, 1)].to_broadcast([P, NCH, CAP]), ALU.mult).then_inc(S["g_ok"], 1)
                    for n in range(2):
                        dve.wait_ge(S["up_full"], 2 * i + 1 + n)
                        cols = bank[n][:, :].rearrange("p (f two) -> p f two", two=2)
                        half = slice(256 * n, 256 * n + 256)
                        ts(sg[:, half], cols[:, :, 0], LIMIT, None, ALU.min).then_inc(S["g_ready"], 1)
                        ts(sl[:, half], cols[:, :, 1], LIMIT, -LIMIT, ALU.min, ALU.max).then_inc(S["up_free"], 1)
                    for n in range(2):
                        half = slice(256 * n, 256 * n + 256)
                        dve.wait_ge(S["up_free"], 2 * i + 2 + n)
                        stt(sl[:, half], sl[:, half], 1.0, sg[:, half], ALU.add, ALU.mult).then_inc(S["gl_ok"], 1)
                        dve.wait_ge(S["gl_ok"], 2 * i + 1 + n)
                        dve.wait_ge(S["sig_ready"], 2 * i + 1 + n)
                        tt(act_h[:, half], sl[:, half], sq[:, half], ALU.mult).then_inc(S["act_ready"], 1)
                    gathered(1 - x, i + 2)
                    dve.wait_ge(S["y_full"], i + 2)
                    dve.tensor_copy(ysb[CAP * x:CAP * x + CAP, 512:1024], bank[4][CAP:2 * CAP, :]).then_inc(S["ysb_ok"], 1)
                for j, (c, hf) in enumerate(CH):
                    r = slice(0, ROWS[c])
                    part = h[r, c, 512 * hf:512 * hf + 512]
                    dve.wait_ge(s_free[j % 3], 2 * q + j // 3 + 1)
                    dve.wait_ge(s_full[j % 3], 2 * q + 2 + j // 3)
                    tt(part, part, bank[5 + j % 3][r, :], ALU.add).then_inc(s_free[j % 3], 1)
            for j in range(3):
                dve.wait_ge(s_free[j], n_pass * NE + 1)
            dve.memset(npf[0:1, 7:8], 0.0).then_inc(S["moe_done"], 1)
            dve.wait_ge(S["rs_p_ok"], 1)
            for c in range(NCH):
                r = slice(0, ROWS[c])
                ts(hn[r, c, :], h[r, c, :], rs_p[r, c:c + 1], None, ALU.mult).then_inc(S["hn_ok"], 1)
            for k in range(2):
                o = filled(dve, ("pT", k))
                dve.tensor_copy(pT[:, k, :], o[:, 0:T]).then_inc(freed(("pT", k)), 1)
            turned("nT", 8, CH)
            for c in range(NCH):
                r = slice(0, ROWS[c])
                for hf in range(2):
                    half = slice(512 * hf, 512 * hf + 512)
                    stored(dve, ("pg", c, hf))
                    stored(dve, ("pp", c, hf))
                    n = put(tt(pgs[r, c, half], pgs[r, c, half], pp[r, c, half], ALU.mult))
                after(n)
                tt(h[r, c, :], h[r, c, :], pgs[r, c, :], ALU.add).then_inc(S["hfin"], 1)
            dve.wait_ge(S["rs_f_ok"], 1)
            dve.wait_ge(S["gf_in"], 16)
            for c in range(NCH):
                r = slice(0, ROWS[c])
                stt(yout[r, c, :], h[r, c, :], rs_f[r, c:c + 1], gfin[r, :], ALU.mult, ALU.mult).then_inc(S["yo_ok"], 1)


_INS = ["x_prompt", "x_sample", "state_ssm", "state_conv", "p_prompt", "p_sample", "norm_mix_g", "w_in", "conv_w",
        "conv_b", "dt_bias", "a_log", "d_skip", "ssd_norm_g", "v_norm_g", "v_norm_b", "w_spatial", "b_spatial",
        "mlp_out_g", "w_out", "norm_moe_g", "w_router", "b_router", "w_up", "b_up", "w_down", "b_down", "norm_ple_g",
        "w_ple_gate", "w_ple_proj", "norm_final_g"]
_OUTS = [("y_prompt", (1, T_PROMPT, D)), ("y_sample", (B_S, L_S, D)),
         ("new_ssm_prompt", (1, 1, HEADS, HD, N_ST)), ("new_conv_prompt", (1, 1, 3, CONV)),
         ("new_ssm_sample", (1, B_S, HEADS, HD, N_ST)), ("new_conv_sample", (1, B_S, 3, CONV)),
         ("new_chunk_v_sample", (1, B_S, L_S, MLP))]


def kernel(**inputs):
    import numpy as _np
    import concourse.bacc as _bacc
    from concourse.bass_utils import run_bass_kernel_spmd as _run

    nc = _bacc.Bacc("TRN2", target_bir_lowering=False, num_devices=1)
    arrays, ins, outs = {}, {}, {}
    for name in _INS:
        a = _np.ascontiguousarray(inputs[name])
        arrays[f"in_{name}_dram"] = a
        ins[name] = nc.dram_tensor(f"in_{name}_dram", a.shape, mybir.dt.from_np(a.dtype), kind="ExternalInput").ap()
    for name, shape in _OUTS:
        outs[name] = nc.dram_tensor(f"out_{name}_dram", shape, F32, kind="ExternalOutput").ap()
    build(nc, ins, outs)
    r = _run(nc, [arrays], core_ids=[0])
    return tuple(r.results[0][f"out_{name}_dram"] for name, _ in _OUTS)
```

```python
from contextlib import ExitStack

import concourse.bass as bass
from concourse import mybir

ALU = mybir.AluOpType
ACT = mybir.ActivationFunctionType
AX_X = mybir.AxisListType.X
F32 = mybir.dt.float32
BF16 = mybir.dt.bfloat16
I32 = mybir.dt.int32

P = 128
D = 1024
KD = D // P
T_PROMPT, B_S, L_S = 256, 8, 4
T_S = B_S * L_S
T = T_PROMPT + T_S
ROWS = [128, 128, T_S]
TOK = [slice(0, 128), slice(128, 256), slice(256, T)]
NCH = 3
ORDER = (2, 0, 1)
SSD, HEADS, HD, GROUPS, HPG, N_ST = 512, 8, 64, 2, 4, 128
CONV = 1024
MLP, MHEADS, MHD = 512, 8, 64
NE, TOPK, FF = 32, 4, 1024
PLE = 256
CAP = 64
PASSES = -(-T // CAP)
NCOL = PASSES * NE + 2
LIMIT, ALPHA, EPS = 7.0, 1.702, 1e-6
NEG = -1e30
BIG = 3e38


def plan_psum():
    both = [(c, hf) for c in range(NCH) for hf in range(2)]
    jobs = [("par", 2, None)]
    jobs += [(("xT", *ch), 1, None) for ch in both]
    jobs += [("dt", 3, None)]
    jobs += [(("xbc", t), 2, None) for t in range(4)]
    jobs += [(("wT", q), 1, None) for q in range(2)] + [("bT", 1, None), ("acum", 2, None)]
    jobs += [(("acb", c, g), 5, None) for c in range(2) for g in range(GROUPS)] + [("acb2", 8, None), ("decs", 1, None)]
    jobs += [(("xbc", t), 2, None) for t in range(4, 8)] + [("rep", 2, None)]
    jobs += [((n, hf), 1, None) for n in ("cvp", "cvs") for hf in range(2)]
    jobs += [(("z", 0), 1, None), (("z", 1), 1, None), ("zuv2", 3, None)]
    jobs += [(("cb", c), 2, None) for c in range(NCH)]
    jobs += [((n, c), 1, None) for c in range(NCH) for n in ("xtm", "btm")]
    jobs += [(("v", 0), 1, None)]
    jobs += [(("st", c), 1, None) for c in range(2)]
    jobs += [(("yd", 0), 1, None), (("yd", 1), 1, None), ("yo1", 1, None), (("yd", 2), 1, None), (("v", 1), 1, None)]
    jobs += [("yos", 4, 6), (("u", 0), 1, 7)]
    jobs += [(("h0T", b), 1, b % 6) for b in range(B_S)]
    six = (0, 1, 2, 3, 4, 5)
    jobs += [("hf", 1, six), (("u", 1), 1, 6)] + [(("ns", t, b), 4, six) for t in range(4) for b in range(2)]
    few, more = (7, 6, 5), (5, 6, 7, 0, 1, 2)
    jobs += [(("cat", c, 0), 1, six) for c in ORDER] + [(("sp", c), 1, few) for c in ORDER]
    jobs += [(("wo", 2), 4, 0)] + [(("wo", c, hf), 1, 1 + 2 * c + hf) for c in range(2) for hf in range(2)]
    jobs += [(("cat", c, 1), 1, few) for c in ORDER]
    turned = lambda c: [(("mT", c, 0), 1, more), (("mT", c, 1), 1, more)]
    jobs += turned(2) + [(("lg", 2), 1, more)]
    jobs += turned(0) + [(("pT", k), 1, more) for k in range(2)] + [(("lg", 0), 1, more), (("pp", 2), 2, more)]
    jobs += turned(1) + [(("pp", 0, 0), 1, more), (("lg", 1), 1, more), (("pp", 0, 1), 1, more), ("pos", 4, more)]
    jobs += [(("pp", 1, 0), 1, 3), (("pp", 1, 1), 1, 4), ("end_moe", 0, None)]
    jobs += [(("nT", c, hf), 1, b + hf) for c, b in ((2, 0), (0, 3), (1, 5)) for hf in range(2)]
    jobs += [(("pg", 2), 2, 7)] + [(("pg", c, hf), 1, 3 * c + hf) for c in range(2) for hf in range(2)]
    place, full, free, turn = {}, [0] * 8, [0] * 8, {}
    for name, reads, bank in jobs:
        if name == "end_moe":
            place[name] = (list(full), list(free))
            continue
        if not isinstance(bank, int):
            banks = bank or tuple(range(8))
            turn[banks] = turn.get(banks, -1) + 1
            bank = banks[turn[banks] % len(banks)]
        place[name] = (bank, full[bank] + 1, free[bank], free[bank] + reads)
        full[bank] += 1
        free[bank] += reads
    return place


def build(nc, I, O):
    PS = plan_psum()
    ctx = ExitStack()
    with ctx:
        def sb(name, shape, dt=F32):
            return ctx.enter_context(nc.sbuf_tensor(name, shape, dt))

        def semaphores(text):
            return {n: ctx.enter_context(nc.semaphore(n)) for n in text.split()}

        ring = sb("ring", [P, 12 * 2048])
        h = sb("h", [P, NCH, D])
        aT = sb("aT", [P, KD, T])
        arena = sb("arena", [P, 21504])
        ident, upper, strict, ones, negm = (sb(n, [P, P]) for n in ("ident", "upper", "strict", "ones", "negm"))
        upper_s, block_s, negm_s = (sb(n, [T_S, T_S]) for n in ("upper_s", "block_s", "negm_s"))
        seq_s = sb("seq_s", [T_S, B_S])
        rep4 = sb("rep4", [L_S, T_S])
        iota = sb("iota", [P, CAP])
        bias_ones = sb("bias_ones", [P, CAP], BF16)
        thr = sb("thr", [1, PASSES - 1])
        pf = sb("pf", [P, KD, 9])
        pb = sb("pb", [P, 3 * HEADS])
        brow = sb("brow", [P, NE])
        wrt = sb("wrt", [P, KD, NE])
        small = sb("small", [P, 12, NCH * HEADS])
        stat = sb("stat", [P, 12, NCH])
        gstat = sb("gstat", [P, 2, 2 * NCH])
        bn = sb("bn", [P, NCH, 6])
        mv = sb("mv", [P, NCH, 2])
        nwt = sb("nwt", [P, 2, 2 * NCH])
        bsp = sb("bsp", [P, MHEADS])
        bss = sb("bss", [T_S, MHEADS])
        decs = sb("decs", [P, 4, B_S])
        npf = sb("npf", [1, 8])
        npi = sb("npi", [1, 1], I32)

        dtr, dta, dtb, dtc, dt, av, acum, atot, eac, dec = (
            small[:, n, :].rearrange("p (c h) -> p c h", c=NCH) for n in range(10))
        aneg = small[:, 10, 0:HEADS]
        edec = small[:, 11, 0:HEADS]
        ss_x, rs_x, ss_m, rs_m, ss_o, rs_o, ss_p, rs_p, ss_f, rs_f, rs_v, ss_f2 = (stat[:, n, :] for n in range(12))
        ss_g, rs_g = gstat[:, 0, :], gstat[:, 1, :]

        def view(at, *dims):
            n = 1
            for x in dims:
                n *= x
            v = arena[:, at:at + n]
            names = "abcd"[:len(dims)]
            return v.rearrange("p (%s) -> p %s" % (" ".join(names), " ".join(names)),
                               **dict(zip(names, dims))) if len(dims) > 1 else v

        xact = view(0, KD, T)
        zs, us, vs = view(2304, NCH, SSD), view(3840, NCH, MLP), view(5376, NCH, MLP)
        xs, xdt = view(6912, NCH, SSD), view(8448, NCH, SSD)
        xn = view(6912, NCH, D)
        xdtd = view(9984, NCH, SSD)
        cvp = view(9984, 1024)
        junk_x = view(9984, 1024)
        btm = view(11520, NCH, 2, N_ST)
        bmask = view(12288, GROUPS, B_S, N_ST)
        cmask = view(14336, GROUPS, B_S, T_S)
        xp = view(12288, KD, T_PROMPT + 3)
        xps = view(12288 + KD * (T_PROMPT + 3), KD, L_S + 3, B_S)
        hs1, hs2 = view(14848, SSD), view(15360, SSD)
        wsp = view(14848, MHEADS, P)
        h0t = view(15872, 2, SSD)
        prow = view(15872, 1024)
        wspT = view(16896, MHEADS, P)
        wsps = view(17920, MHEADS, B_S, L_S)
        vgb = view(18176, 2, MLP)
        bup_f, bup_r = ring[:, 20544:21312], ring[:, 22528:23296]
        bup_p = ring[:, 23296:24448].bitcast(BF16).rearrange("p (t n) -> p t n", t=3)
        cvs = view(19968, 1024)
        aex = view(19968, 512)
        junk = view(19968, 512)
        yoff = view(20992, 512)
        seqm = view(20992, B_S, T_S)
        bsn = view(11008, P)
        lmat = [view(3840, HEADS, P), view(15872, HEADS, P)]
        lmat_s = view(19200, HEADS, T_S)[0:T_S]
        mbf = view(0, 4608).bitcast(BF16).rearrange("p (c t n) -> p c t n", c=NCH, t=3)
        mn = view(4608, NCH, D)
        mr = view(7680, NCH, D)
        xT = view(7680, 2, KD, CAP)
        sg, sl, sq = view(8704, 512), view(9216, 512), view(9728, 512)
        act_h = view(10240, 512)
        actT = view(10752, 4, 2, CAP)
        ysb = view(11264, D)
        gsel = view(12288, NCH, P)
        gselT = view(12672, T)
        sel = view(12960, 192).bitcast(BF16).rearrange("p (x c s) -> p x c s", x=2, c=NCH)
        pos_t, gate_t = view(16224, NCH, NCOL), view(16710, NCH, NCOL)
        lgt, mrep, msk, gat, ex, prk = (view(17196 + 120 * n, NCH, 40) for n in range(6))
        top8, top4 = view(17916, NCH, 8), view(17940, NCH, 8)
        gsum, grec = view(17964, NCH), view(17967, NCH)
        w_pp = view(10752, 2, D)
        prows = view(14688, NCH, PLE)
        pT = view(15456, 2, T)
        pp = view(17980, NCH, D)
        part_rows = [slice(T_S * (x + 1), T_S * (x + 1) + 3) for x in range(2)]
        b_up3 = [h[r, 2, :].bitcast(BF16) for r in part_rows]
        b_down3 = [pp[r, 2, 0:D // 2].bitcast(BF16) for r in part_rows]
        pgs = view(10240, NCH, D)
        gfin = view(7680, D)
        yout = view(13312, NCH, D)

        w_xbc = ring[:, 0:8192].rearrange("p (k n) -> p k n", k=KD)
        w_zuv = [ring[:, 8192 + 4096 * n:12288 + 4096 * n].rearrange("p (k n) -> p k n", k=KD) for n in range(3)]
        w_o = ring[:, 0:8192].rearrange("p (k n) -> p k n", k=KD)
        w_dt = ring[:, 20480:20544].rearrange("p (k n) -> p k n", k=KD)
        h0 = ring[:, 20480:24576].rearrange("p (b t n) -> p b t n", b=B_S, t=4)
        w_pg = ring[:, 0:8192].rearrange("p (k n) -> p k n", k=KD)

        apart = [[view(13152, 1024), view(14176, 1024)],
                 [view(4608, 1024), view(5632, 1024)],
                 [aT[:, :, :].rearrange("p k t -> p (k t)")[:, 1024 * f:1024 * f + 1024] for f in range(2)],
                 [view(6656, 1024), view(15200, 1024)]]

        def slot(s):
            return ring[:, 2048 * s:2048 * (s + 1)]

        def halves(s, x):
            return apart[s] if x and s < len(apart) else [slot(s)[:, 1024 * f:1024 * f + 1024] for f in range(2)]

        bank = [ctx.enter_context(nc.psum_tensor(f"bank{b}", [P, 512], F32)) for b in range(8)]
        bup_split = nc.dram_tensor("bup_split", [3, NE, 2 * FF + D], BF16, kind="Internal").ap()

        bank_full = [ctx.enter_context(nc.semaphore(f"bank_full{b}")) for b in range(8)]
        bank_free = [ctx.enter_context(nc.semaphore(f"bank_free{b}")) for b in range(8)]
        S = semaphores(
            "a_ok ach act_ready aex_ok anexp at_free at_full bmask_ok brow_in bs_in bup_in "
            "bup_parts bup_stored cmask_ok consts conv_ok cv_out dec_in dt dt_in dtabs dtadd dtexp dtln "
            "eac_ok end_moe fin_ss fss g_ok g_ready gex gf_in gl_ok h0_in h0t_used hf_out hfin hss ident_ok "
            "lexp m1_ok m2_ok m3_ok m_ok mask_ok mbf_zero mix_done mix_ok mn_ok moe_done mss ngm_ok npass_ok "
            "ns_out pads par_in pb_in pch pg_sig pg_sum pr_in r1_ok rs_p_ok sel_ok sig_ready sumsq tables "
            "u_in up_free up_full v_in v_out vch vgb_in vinit vn_ok w_used wmask wo_half wo_in wrt_in wsp_in "
            "xact_ok xdtd_ok xn_ok xt_full xt_ready y_full y_ok y_out ygs yn_ok yo_ok ysb_ok z_in")
        xbc_in = [ctx.enter_context(nc.semaphore(f"xbc_in{q}")) for q in range(4)]
        x_in = [ctx.enter_context(nc.semaphore(f"x_in{c}")) for c in range(NCH)]
        bias_in = [ctx.enter_context(nc.semaphore(f"bias_in{x}")) for x in range(2)]
        pw_in = [ctx.enter_context(nc.semaphore(f"pw_in{q}")) for q in range(2)]
        w_full = [ctx.enter_context(nc.semaphore(f"w_full{s}")) for s in range(12)]
        w_full_apart = [ctx.enter_context(nc.semaphore(f"w_full_apart{s}")) for s in range(len(apart))]
        s_full = [ctx.enter_context(nc.semaphore(f"s_full{s}")) for s in range(3)]
        s_free = [ctx.enter_context(nc.semaphore(f"s_free{s}")) for s in range(3)]

        SCATTER = [(2, None), (0, 0), (0, 1), (1, 0), (1, 1)]
        S_JOBS = [2, 2, 1]
        S_READS = [3, 2, 1]

        def filled(eng, name):
            b, full, _, _ = PS[name]
            eng.wait_ge(bank_full[b], full)
            return bank[b]

        def stored(eng, name):
            b, _, _, after = PS[name]
            eng.wait_ge(bank_free[b], after)

        def scatter_reads(j):
            return sum(2 if SCATTER[m][0] == 2 else 1 for m in range(j % 3, j + 1, 3))

        def experts_done(eng, n_pass, c):
            for j, (cj, _) in enumerate(SCATTER):
                if cj == c:
                    left = S_READS[j % 3] - scatter_reads(j)
                    eng.wait_ge(s_free[j % 3], n_pass * (NE // 2 * S_READS[j % 3]) - left + 1)

        def freed(name):
            return bank_free[PS[name][0]]

        BANK_END = PS["end_moe"]
        N_CONST = 10

        CH = [(c, hf) for c in range(NCH) for hf in range(2)]
        hs3 = lambda ap: ap.rearrange("p (h d) -> p h d", d=HD)

        def over(ap, shape):
            return ap.unsqueeze(2).to_broadcast(shape)

        block = ctx.enter_context(nc.Block())

        @block.sync
        def _(sp):
            xr = I["x_prompt"].rearrange("a (c p) d -> p (a c) d", p=P)
            sp.dma_start(h[:, 0, :], xr[:, 0, :]).then_inc(x_in[0], 16)
            sp.dma_start(h[:, 1, :], xr[:, 1, :]).then_inc(x_in[1], 16)
            sp.dma_start(h[0:T_S, 2, :], I["x_sample"].rearrange("b s d -> (b s) d")).then_inc(x_in[2], 16)
            sp.wait_ge(S["par_in"], 16 * 8)
            w_in = I["w_in"][0].rearrange("(k p) n -> p k n", p=P)
            o = SSD + CONV
            with nc.allow_non_contiguous_dma(reason="eight dt columns"):
                sp.dma_start(w_dt, w_in[:, :, o:o + HEADS]).then_inc(S["dt_in"], 16)
            for q in range(4):
                sp.dma_start(w_xbc[:, 2 * q:2 * q + 2, :], w_in[:, 2 * q:2 * q + 2, SSD:o]).then_inc(xbc_in[q], 16)
            sp.dma_start(wsp, I["w_spatial"][0].rearrange("h i j -> i h j")).then_inc(S["wsp_in"], 16)
            sp.dma_start(bsn[0:MHEADS, :], I["b_spatial"][0]).then_inc(S["bs_in"], 16)
            sp.dma_start(brow[:, :], I["b_router"][0].partition_broadcast(P)).then_inc(S["brow_in"], 16)
            sp.dma_start(w_zuv[0], w_in[:, :, 0:SSD]).then_inc(S["z_in"], 16)
            bu = I["b_up"][0].rearrange("e (q n) -> (e q) n", n=512)
            sp.dma_start(bup_f[:, 0:512], bu).then_inc(S["bup_in"], 16)
            sp.dma_start(bup_f[:, 512:768], I["b_down"][0].rearrange("e (q n) -> (e q) n", n=256)).then_inc(S["bup_in"], 16)
            sp.dma_start(w_zuv[1], w_in[:, :, o + HEADS:o + HEADS + MLP]).then_inc(S["u_in"], 16)
            sp.dma_start(w_zuv[2], w_in[:, :, o + HEADS + MLP:o + HEADS + 2 * MLP]).then_inc(S["v_in"], 16)
            sp.dma_start(vgb[:, 0, :], I["v_norm_g"][0].partition_broadcast(P)).then_inc(S["vgb_in"], 16)
            sp.dma_start(vgb[:, 1, :], I["v_norm_b"][0].partition_broadcast(P)).then_inc(S["vgb_in"], 16)
            sp.dma_start(wrt[:, :, :], I["w_router"][0].rearrange("(k p) n -> p k n", p=P)).then_inc(S["wrt_in"], 16)
            sp.wait_ge(S["bup_stored"], 96)
            b, full, _, _ = PS["dt"]
            sp.wait_ge(bank_full[b], full)
            sp.dma_start(h0, I["state_ssm"][0].rearrange("b h q n -> b (h q) n").rearrange("b (t p) n -> p b t n", p=P))\
              .then_inc(S["h0_in"], 16)
            b, full, _, _ = PS[("xbc", 7)]
            sp.wait_ge(bank_full[b], full)
            sp.dma_start(w_o, I["w_out"][0].rearrange("(k p) n -> p k n", p=P)).then_inc(S["wo_in"], 16)

            def up_tile(e, s):
                return I["w_up"][0, e, s * P:(s + 1) * P, :]

            def down_tile(e, s):
                return I["w_down"][0, e, 2 * s * P:(2 * s + 2) * P, :].rearrange("(a p) n -> p a n", p=P)

            order = [4, 5, 8, 9, 6, 7, 0, 1, 2, 3, 10, 11]
            behind = {4: "zuv2", 8: ("v", 1), 6: ("u", 1), 2: ("wo", 1, 1)}
            for s in order:
                if s in behind:
                    b, full, _, _ = PS[behind[s]]
                    sp.wait_ge(bank_full[b], full)
                if s == 0:
                    sp.wait_ge(S["wo_half"], 1)
                if s == 10:
                    sp.wait_ge(S["ns_out"], 16)
                if s < 8:
                    sp.dma_start(slot(s), up_tile(0, s)).then_inc(w_full[s], 16)
                else:
                    sp.dma_start(slot(s).rearrange("p (a n) -> p a n", a=2), down_tile(0, s - 8)).then_inc(w_full[s], 16)
            def fetch_bias(e, x):
                parts = bup_split[:, bass.ds(e, 1), :].rearrange("t a n -> (t a) n")
                sp.dma_start(b_up3[x], parts[:, 0:2 * FF]).then_inc(bias_in[x], 16)
                sp.dma_start(b_down3[x], parts[:, 2 * FF:]).then_inc(bias_in[x], 16)

            sp.wait_ge(S["mix_done"], 1)
            fetch_bias(0, 0)

            def fetch(i, e, x, first=False):
                if not first:
                    sp.wait_ge(S["w_used"], 10 * i - 9)
                fetch_bias(e, x)
                for s in range(12):
                    if s < len(apart):
                        if first:
                            if s == 1:
                                sp.wait_ge(S["r1_ok"], 3)
                            for name in ([("pT", 1)], [("mT", 1, 0), ("mT", 1, 1)], [("lg", 1)], [("pp", 1, 1)])[s]:
                                b, full, _, _ = PS[name]
                                sp.wait_ge(bank_full[b], full)
                        else:
                            sp.wait_ge(S["w_used"], 10 * i - 20 + s + 1)
                    elif s == 7:
                        sp.wait_ge(S["up_full"], 2 * i)
                    elif s == 11:
                        sp.wait_ge(S["y_full"], i + 1)
                    else:
                        sp.wait_ge(S["w_used"], 10 * i - 10 + s + (s < 8))
                    if s < 8:
                        src = I["w_up"][0, bass.ds(e, 1), s * P:(s + 1) * P, :].rearrange("a p n -> (a p) n")
                        if s < len(apart) and x:
                            for f in range(2):
                                sp.dma_start(apart[s][f], src[:, 1024 * f:1024 * f + 1024]).then_inc(w_full_apart[s], 16)
                        else:
                            sp.dma_start(slot(s), src).then_inc(w_full[s], 16)
                    else:
                        k = s - 8
                        src = I["w_down"][0, bass.ds(e, 1), 2 * k * P:(2 * k + 2) * P, :]
                        sp.dma_start(slot(s).rearrange("p (a n) -> p a n", a=2),
                                     src.rearrange("e (a p) n -> p (e a) n", p=P)).then_inc(w_full[s], 16)

            fetch(1, 1, 1, first=True)
            with sp.Fori(1, NE // 2) as q:
                for x in range(2):
                    fetch(2 * q + x, 2 * q + x, x)
            sp.wait_ge(S["npass_ok"], 1)
            n_pass = sp.value_load(npi[0:1, 0:1], min_val=1, max_val=PASSES)
            with sp.If(n_pass > 1):
                with sp.Fori(1, n_pass) as r:
                    with sp.Fori(0, NE // 2) as q:
                        for x in range(2):
                            fetch(r * NE + 2 * q + x, 2 * q + x, x)
            sp.wait_ge(S["up_full"], n_pass * (2 * NE))
            wpg = I["w_ple_gate"][0].rearrange("(k p) n -> p k n", p=P)
            for q in range(2):
                sp.dma_start(w_pg[:, 4 * q:4 * q + 4, :], wpg[:, 4 * q:4 * q + 4, :]).then_inc(pw_in[q], 16)
            sp.wait_ge(S["moe_done"], 1)
            sp.dma_start(gfin, I["norm_final_g"].partition_broadcast(P)).then_inc(S["gf_in"], 16)
            ypr = O["y_prompt"].rearrange("a (c p) d -> p (a c) d", p=P)
            for n, c in enumerate(ORDER):
                for hf in range(2):
                    half = slice(512 * hf, 512 * hf + 512)
                    sp.wait_ge(S["yo_ok"], 2 * n + hf + 1)
                    if c < 2:
                        sp.dma_start(ypr[:, c, half], yout[:, c, half]).then_inc(S["y_out"], 16)
                    else:
                        sp.dma_start(O["y_sample"].rearrange("b s d -> (b s) d")[:, half], yout[0:T_S, 2, half])\
                          .then_inc(S["y_out"], 16)
            sp.wait_ge(S["y_out"], 32 * NCH)

        @block.gpsimd
        def _(pool):
            n_done = [0]

            def step(ins):
                n_done[0] += 1
                ins.then_inc(S["pch"], 1)
                pool.wait_ge(S["pch"], n_done[0])

            pool.dma_start(pb[:, 0:HEADS], I["dt_bias"][0].partition_broadcast(P)).then_inc(S["pb_in"], 16)
            pool.dma_start(pb[:, HEADS:2 * HEADS], I["a_log"][0].partition_broadcast(P)).then_inc(S["pb_in"], 16)
            pool.dma_start(pb[:, 2 * HEADS:], I["d_skip"][0].partition_broadcast(P)).then_inc(S["pb_in"], 16)
            step(pool.memset(ident[:, :], 0.0))
            pool.affine_select(out=ident[:, :], in_=ident[:, :], compare_op=ALU.not_equal, fill=1.0,
                               base=0, pattern=[[-1, P]], channel_multiplier=1).then_inc(S["ident_ok"], 1)
            pool.memset(xp[:, :, 0:3], 0.0).then_inc(S["pads"], 1)
            step(pool.memset(ones[:, :], 1.0))
            pool.affine_select(out=upper[:, :], in_=ones[:, :], compare_op=ALU.is_ge, fill=0.0,
                               base=0, pattern=[[1, P]], channel_multiplier=-1).then_inc(S["consts"], 1)
            pool.affine_select(out=strict[:, :], in_=ones[:, :], compare_op=ALU.is_ge, fill=0.0,
                               base=-1, pattern=[[1, P]], channel_multiplier=-1).then_inc(S["consts"], 1)
            step(pool.memset(negm[:, :], 0.0))
            pool.affine_select(out=negm[:, :], in_=negm[:, :], compare_op=ALU.is_ge, fill=NEG,
                               base=0, pattern=[[1, P]], channel_multiplier=-1).then_inc(S["consts"], 1)
            bb = block_s[:, :].rearrange("p (b s) -> p b s", b=B_S)
            one_s = ones[0:T_S, 0:T_S].rearrange("p (b s) -> p b s", b=B_S)
            step(pool.affine_select(out=bb, in_=one_s, compare_op=ALU.is_ge, fill=0.0, base=0,
                                    pattern=[[-L_S, B_S], [0, L_S]], channel_multiplier=1))
            step(pool.affine_select(out=bb, in_=bb, compare_op=ALU.is_ge, fill=0.0, base=L_S - 1,
                                    pattern=[[L_S, B_S], [0, L_S]], channel_multiplier=-1))
            step(pool.affine_select(out=upper_s[:, :], in_=block_s[:, :], compare_op=ALU.is_ge, fill=0.0,
                                    base=0, pattern=[[1, T_S]], channel_multiplier=-1))
            pool.tensor_scalar(negm_s[:, :], upper_s[:, :], -1.0, -NEG, ALU.add, ALU.mult).then_inc(S["consts"], 1)
            step(pool.affine_select(out=seq_s[:, :], in_=ones[0:T_S, 0:B_S], compare_op=ALU.is_ge, fill=0.0, base=0,
                                    pattern=[[-L_S, B_S]], channel_multiplier=1))
            pool.affine_select(out=seq_s[:, :], in_=seq_s[:, :], compare_op=ALU.is_ge, fill=0.0, base=L_S - 1,
                               pattern=[[L_S, B_S]], channel_multiplier=-1).then_inc(S["consts"], 1)
            step(pool.memset(rep4[:, :], 0.0))
            r4 = rep4[:, :].rearrange("p (b s) -> p b s", b=B_S)
            pool.affine_select(out=r4, in_=r4, compare_op=ALU.not_equal, fill=1.0, base=0,
                               pattern=[[0, B_S], [1, L_S]], channel_multiplier=-1).then_inc(S["consts"], 1)
            pool.iota(iota[:, :], pattern=[[1, CAP]], base=0, channel_multiplier=0,
                      allow_small_or_imprecise_dtypes=True).then_inc(S["consts"], 1)
            pool.memset(bias_ones[:, :], 1.0).then_inc(S["consts"], 1)
            pool.iota(thr[:, :], pattern=[[CAP, PASSES - 1]], base=CAP, channel_multiplier=0,
                      allow_small_or_imprecise_dtypes=True).then_inc(S["consts"], 1)
            one_m = ones[:, 0:T_S].unsqueeze(1).to_broadcast([P, B_S, T_S])
            step(pool.affine_select(out=seqm, in_=one_m, compare_op=ALU.is_ge, fill=0.0, base=0,
                                    pattern=[[-L_S, B_S], [1, T_S]], channel_multiplier=0))
            pool.affine_select(out=seqm, in_=seqm, compare_op=ALU.is_ge, fill=0.0, base=L_S - 1,
                               pattern=[[L_S, B_S], [-1, T_S]], channel_multiplier=0).then_inc(S["consts"], 1)
            pool.wait_ge(S["wsp_in"], 16)
            pool.affine_select(out=wsp, in_=wsp, compare_op=ALU.is_ge, fill=0.0, base=0,
                               pattern=[[0, MHEADS], [-1, P]], channel_multiplier=1).then_inc(S["wmask"], 1)
            pool.wait_ge(S["bup_in"], 32)
            step(pool.tensor_copy(bup_p[:, 0, :], bup_f))
            step(pool.tensor_tensor(bup_r, bup_f, bup_p[:, 0, :], ALU.subtract))
            step(pool.tensor_copy(bup_p[:, 1, :], bup_r))
            step(pool.tensor_tensor(bup_f, bup_r, bup_p[:, 1, :], ALU.subtract))
            pool.tensor_copy(bup_p[:, 2, :], bup_f).then_inc(S["bup_parts"], 1)
            pool.wait_ge(S["bup_parts"], 1)
            for t in range(3):
                pool.dma_start(bup_split[t, :, 0:2 * FF].rearrange("e (q n) -> e q n", n=512), bup_p[:, t, 0:512])\
                    .then_inc(S["bup_stored"], 16)
                pool.dma_start(bup_split[t, :, 2 * FF:].rearrange("e (q n) -> e q n", n=256), bup_p[:, t, 512:768])\
                    .then_inc(S["bup_stored"], 16)
            for n in ("cvp", "cvs"):
                for hf in range(2):
                    stored(pool, (n, hf))
            pool.dma_start(O["new_conv_prompt"][0, 0], cvp[T_S - 3:T_S, :]).then_inc(S["cv_out"], 16)
            for t in range(1, L_S):
                pool.dma_start(O["new_conv_sample"][0, :, t - 1, :], cvs[B_S * t:B_S * t + B_S, :]).then_inc(S["cv_out"], 16)
            pool.wait_ge(S["cv_out"], 16 * L_S)
            pool.wait_ge(S["vn_ok"], 3)
            pool.dma_start(O["new_chunk_v_sample"][0].rearrange("b s d -> (b s) d"), vs[0:T_S, 2, :])\
                .then_inc(S["v_out"], 16)
            stored(pool, "hf")
            pool.dma_start(O["new_ssm_prompt"][0, 0].rearrange("h q n -> (h q) n").rearrange("(t p) n -> p t n", p=P),
                           xdt[:, 0, :].rearrange("p (t n) -> p t n", t=4)).then_inc(S["hf_out"], 16)
            for t in range(4):
                for bh in range(2):
                    stored(pool, ("ns", t, bh))
            pool.dma_start(w_pp, I["w_ple_proj"][0].rearrange("(k p) n -> p k n", p=P)).then_inc(S["pr_in"], 16)
            pool.dma_start(O["new_ssm_sample"][0].rearrange("b h q n -> b (h q) n").rearrange("b (t p) n -> p b t n", p=P),
                           h0).then_inc(S["ns_out"], 16)
            pool.wait_ge(S["mix_done"], 1)
            pool.dma_start(prows[:, 0:2, :], I["p_prompt"][0].rearrange("a (c p) d -> p (a c) d", p=P))\
                .then_inc(S["pr_in"], 16)
            pool.dma_start(prows[0:T_S, 2, :], I["p_sample"][0].rearrange("b s d -> (b s) d")).then_inc(S["pr_in"], 16)
            pool.memset(mbf[:, 2, :, :], 0.0).then_inc(S["mbf_zero"], 1)
            pool.memset(lgt, BIG).then_inc(S["tables"], 1)
            for table, value in ((top4, BIG), (gat, 0.0), (prk, 0.0), (pos_t, -1.0), (gate_t, 0.0)):
                pool.memset(table, value).then_inc(S["tables"], 1)
            filled(pool, ("pp", 1, 1))
            pool.memset(gsel, 0.0).then_inc(S["tables"], 1)
            pool.wait_ge(S["v_out"], 16)
            pool.wait_ge(S["hf_out"], 16)
            pool.wait_ge(S["ns_out"], 16)

        @block.tensor
        def _(pe):
            def open_bank(name):
                b, _, before, _ = PS[name]
                if before:
                    pe.wait_ge(bank_free[b], before)
                return bank[b]

            def close_bank(name, mm):
                mm.then_inc(bank_full[PS[name][0]], 1)

            pe.wait_ge(S["ident_ok"], 1)
            pe.wait_ge(S["par_in"], 16 * 8)
            o = open_bank("par")
            for k in range(KD):
                mm = pe.transpose(o[:, 33 * k:33 * k + 33], prow[0:33, k * P:(k + 1) * P], ident[0:33, 0:33])
            close_bank("par", mm)

            def transposed(name, src, c, k0=0):
                o = open_bank(name)
                for j in range(4):
                    k = k0 + j
                    mm = pe.transpose(o[:, j * ROWS[c]:(j + 1) * ROWS[c]], src[0:ROWS[c], c, k * P:(k + 1) * P],
                                      ident[0:ROWS[c], 0:ROWS[c]])
                close_bank(name, mm)

            def rows_product(tag, c, w, ks=range(KD), first=True, last=True, src=aT, halves=(0, 1), split=False):
                for hf in ((None,) if c == 2 else halves):
                    name = (tag, 2) if c == 2 else (tag, c, hf)
                    o = open_bank(name) if first else bank[PS[name][0]]
                    sums = 2 if split and c == 2 else 1
                    for k in ks:
                        start, stop = first and k - ks[0] < sums, last and ks[-1] - k < sums
                        for f in ((0, 1) if c == 2 else (hf,)):
                            at = T_S * (2 * (k % sums) + f)
                            out = o[at:at + T_S, :] if c == 2 else o[:, :]
                            mm = pe.matmul(out, src[:, k, TOK[c]], w[:, k, 512 * f:512 * f + 512], start=start, stop=stop)
                    if last:
                        close_bank(name, mm)
                return mm

            for c in range(NCH):
                pe.wait_ge(S["xn_ok"], c + 1)
                for hf in range(2):
                    transposed(("xT", c, hf), xn, c, 4 * hf)
            for c in range(NCH):
                for hf in range(2):
                    stored(pe, ("xT", c, hf))
            pe.wait_ge(S["dt_in"], 16)
            dt_bank = open_bank("dt")

            def project_xbc(ts):
                for t in ts:
                    o = open_bank(("xbc", t))
                    for k in range(KD):
                        if t < NCH:
                            mm = pe.matmul(dt_bank[0:ROWS[t], 8 * t:8 * t + 8], aT[:, k, TOK[t]], w_dt[:, k, :],
                                           start=(k == 0), stop=(k == KD - 1))
                            if t == NCH - 1 and k == KD - 1:
                                close_bank("dt", mm)
                        pe.wait_ge(xbc_in[k // 2], 16)
                        mm = pe.matmul(o[:, 0:T], w_xbc[:, k, t * P:(t + 1) * P], aT[:, k, :],
                                       start=(k == 0), stop=(k == KD - 1))
                    close_bank(("xbc", t), mm)

            project_xbc(range(4))
            pe.wait_ge(S["wmask"], 1)
            for q in range(2):
                o = open_bank(("wT", q))
                for j in range(4):
                    mm = pe.transpose(o[:, j * P:(j + 1) * P], wsp[:, 4 * q + j, :], ident[:, :])
                close_bank(("wT", q), mm)
            pe.wait_ge(S["bs_in"], 16)
            o = open_bank("bT")
            close_bank("bT", pe.transpose(o[:, 0:MHEADS], bsn[0:MHEADS, :], ident[0:MHEADS, 0:MHEADS]))
            pe.wait_ge(S["consts"], N_CONST)
            pe.wait_ge(S["a_ok"], 1)
            o = open_bank("acum")
            for c in range(2):
                pe.matmul(o[:, 8 * c:8 * c + 8], upper[:, :], av[:, c, :], start=True, stop=True)
            pe.matmul(o[0:T_S, 16:24], upper_s[:, :], av[0:T_S, 2, :], start=True, stop=True)
            mm = pe.matmul(o[0:T_S, 24:32], block_s[:, :], av[0:T_S, 2, :], start=True, stop=True)
            close_bank("acum", mm)
            for c in range(2):
                for g in range(GROUPS):
                    o = open_bank(("acb", c, g))
                    for j in range(HPG):
                        hh = HPG * g + j
                        mm = pe.matmul(o[:, j * P:(j + 1) * P], av[:, c, hh:hh + 1].to_broadcast([P, P]), upper[:, :],
                                       start=True, stop=True)
                    close_bank(("acb", c, g), mm)
            o = open_bank("acb2")
            for hh in range(HEADS):
                mm = pe.matmul(o[0:T_S, hh * T_S:(hh + 1) * T_S], av[0:T_S, 2, hh:hh + 1].to_broadcast([T_S, T_S]),
                               upper_s[:, :], start=True, stop=True)
            close_bank("acb2", mm)
            pe.wait_ge(S["aex_ok"], 1)
            o = open_bank("decs")
            for t in range(4):
                mm = pe.matmul(o[:, 8 * t:8 * t + 8], aex[0:T_S, t * P:(t + 1) * P], seq_s[:, :], start=True, stop=True)
            close_bank("decs", mm)
            project_xbc(range(4, 8))
            for n in (("wT", 0), ("wT", 1), "bT"):
                stored(pe, n)
            o = open_bank("rep")
            pe.matmul(o[0:T_S, 0:32], rep4[:, :], wspT[0:L_S, :, 0:L_S], start=True, stop=True)
            mm = pe.matmul(o[0:T_S, 32:40], rep4[:, :], bsp[0:L_S, :], start=True, stop=True)
            close_bank("rep", mm)

            for t in range(8):
                stored(pe, ("xbc", t))
            for n in ("cvp", "cvs"):
                for hf in range(2):
                    o = open_bank((n, hf))
                    for j in range(4):
                        k = 4 * hf + j
                        src = xp[:, k, T_PROMPT + 3 - T_S:T_PROMPT + 3] if n == "cvp" \
                            else xps[:, k, 3:L_S + 3, :].rearrange("p s b -> p (s b)")
                        mm = pe.transpose(o[0:T_S, j * P:(j + 1) * P], src, ident[:, :])
                    close_bank((n, hf), mm)

            def project_step(tag, n, c, k):
                if k == 0:
                    pe.wait_ge(S[tag + "_in"], 16)
                    open_bank((tag, c))
                mm = pe.matmul(bank[PS[(tag, c)][0]][:, :], aT[:, k, TOK[c]], w_zuv[n][:, k, :],
                               start=(k == 0), stop=(k == KD - 1))
                if k == KD - 1:
                    close_bank((tag, c), mm)

            def project(tag, n, c):
                for k in range(KD):
                    project_step(tag, n, c, k)

            project("z", 0, 0)
            project("z", 0, 1)
            pe.wait_ge(S["u_in"], 16)
            pe.wait_ge(S["v_in"], 16)
            o = open_bank("zuv2")
            for k in range(KD):
                for n in range(3):
                    mm = pe.matmul(o[T_S * n:T_S * n + T_S, :], aT[:, k, TOK[2]], w_zuv[n][:, k, :],
                                   start=(k == 0), stop=(k == KD - 1))
            close_bank("zuv2", mm)
            pe.wait_ge(S["xact_ok"], 8)
            for c in range(NCH):
                o = open_bank(("cb", c))
                for g in range(GROUPS):
                    mm = pe.matmul(o[0:ROWS[c], g * P:g * P + ROWS[c]], xact[:, 4 + g, TOK[c]], xact[:, 6 + g, TOK[c]],
                                   start=True, stop=True)
                close_bank(("cb", c), mm)
            for c in range(NCH):
                for n, k0, kn in (("xtm", 0, 4), ("btm", 4, 2)):
                    o = open_bank((n, c))
                    for j in range(kn):
                        mm = pe.transpose(o[0:ROWS[c], j * P:(j + 1) * P], xact[:, k0 + j, TOK[c]], ident[:, :])
                    close_bank((n, c), mm)
            project("v", 2, 0)
            for c in range(2):
                stored(pe, ("btm", c))
                pe.wait_ge(S["xdtd_ok"], c + 1)
                o = open_bank(("st", c))
                for g in range(GROUPS):
                    mm = pe.matmul(o[:, 256 * g:256 * g + 256], btm[:, c, g, :], xdtd[:, c, 256 * g:256 * g + 256],
                                   start=True, stop=True)
                close_bank(("st", c), mm)

            def y_diag(c):
                stored(pe, ("cb", c))
                o = open_bank(("yd", c))
                for hh in range(HEADS):
                    lt = lmat[c][:, hh, :] if c < 2 else lmat_s[:, hh, :]
                    mm = pe.matmul(o[0:ROWS[c], hh * HD:(hh + 1) * HD], lt, xdt[0:ROWS[c], c, hh * HD:(hh + 1) * HD],
                                   start=True, stop=True)
                close_bank(("yd", c), mm)

            y_diag(0)
            y_diag(1)
            stored(pe, ("st", 0))
            o = open_bank("yo1")
            for g in range(GROUPS):
                mm = pe.matmul(o[:, 256 * g:256 * g + 256], xact[:, 6 + g, TOK[1]], hs1[:, 256 * g:256 * g + 256],
                               start=True, stop=True)
            close_bank("yo1", mm)
            pe.wait_ge(S["xdtd_ok"], 3)
            y_diag(2)
            project("v", 2, 1)
            yos = open_bank("yos")
            pe.wait_ge(S["h0_in"], 16)
            pe.wait_ge(S["cmask_ok"], 2)

            def h0_rows(b):
                o = open_bank(("h0T", b))
                for t in range(4):
                    mm = pe.transpose(o[:, t * P:(t + 1) * P], h0[:, b, t, :], ident[:, :])
                close_bank(("h0T", b), mm)

            h0_rows(0)
            for b in range(B_S):
                if b + 1 < B_S:
                    h0_rows(b + 1)
                project_step("u", 1, 0, b)
                stored(pe, ("h0T", b))
                for g in range(GROUPS):
                    at = T_S * (2 * (b % 2) + g)
                    mm = pe.matmul(yos[at:at + T_S, 0:256], cmask[:, g, b, :], h0t[:, b % 2, 256 * g:256 * g + 256],
                                   start=(b < 2), stop=(b >= B_S - 2))
                if b < B_S - 1:
                    mm.then_inc(S["h0t_used"], 1)
                else:
                    close_bank("yos", mm)
            stored(pe, ("st", 1))
            o = open_bank("hf")
            for t in range(4):
                mm = pe.transpose(o[:, t * P:(t + 1) * P], hs2[:, t * P:(t + 1) * P], ident[:, :])
            close_bank("hf", mm)
            pe.wait_ge(S["bmask_ok"], 2)
            for t in range(4):
                for bh in range(2):
                    o = open_bank(("ns", t, bh))
                    mm = pe.matmul(o[:, :], xdtd[0:T_S, 2, t * P:(t + 1) * P],
                                   bmask[0:T_S, t // 2, 4 * bh:4 * bh + 4, :], start=True, stop=True)
                    close_bank(("ns", t, bh), mm)
                    project_step("u", 1, 1, 2 * t + bh)
            for n, c in enumerate(ORDER):
                pe.wait_ge(S["yn_ok"], 2 * n + 2)
                transposed(("cat", c, 0), xs, c)
            stored(pe, "rep")
            for n, c in enumerate(ORDER):
                pe.wait_ge(S["vn_ok"], n + 1)
                o = open_bank(("sp", c))
                for hh in range(MHEADS):
                    lt = wspT[:, hh, :] if c < 2 else wsps[0:T_S, hh, :, :]
                    mm = pe.matmul(o[0:ROWS[c], hh * MHD:(hh + 1) * MHD], lt, vs[0:ROWS[c], c, hh * MHD:(hh + 1) * MHD],
                                   start=True, stop=True)
                close_bank(("sp", c), mm)
            pe.wait_ge(S["wo_in"], 16)
            for c in ORDER:
                stored(pe, ("cat", c, 0))
                mm = rows_product("wo", c, w_o, range(4), last=False, split=True)
            mm.then_inc(S["wo_half"], 1)
            for n, c in enumerate(ORDER):
                pe.wait_ge(S["m_ok"], n + 1)
                transposed(("cat", c, 1), us, c)

            def out_product(c):
                stored(pe, ("cat", c, 1))
                rows_product("wo", c, w_o, range(4, 8), first=False, split=True)

            def turn_rows(n, c):
                pe.wait_ge(S["mn_ok"], n + 1)
                transposed(("mT", c, 0), mn, c)
                transposed(("mT", c, 1), mn, c, 4)

            def logits(c):
                stored(pe, ("mT", c, 0))
                stored(pe, ("mT", c, 1))
                o = open_bank(("lg", c))
                for k in range(KD):
                    mm = pe.matmul(o[0:ROWS[c], 0:NE], aT[:, k, TOK[c]], wrt[:, k, :],
                                   start=(k == 0), stop=(k == KD - 1))
                close_bank(("lg", c), mm)

            out_product(2)
            out_product(0)
            pe.wait_ge(S["wrt_in"], 16)
            turn_rows(0, 2)
            logits(2)
            out_product(1)
            turn_rows(1, 0)
            pe.wait_ge(S["pr_in"], 48)
            for k in range(2):
                o = open_bank(("pT", k))
                for c in range(NCH):
                    mm = pe.transpose(o[:, TOK[c]], prows[0:ROWS[c], c, k * P:(k + 1) * P], ident[0:ROWS[c], 0:ROWS[c]])
                close_bank(("pT", k), mm)
            logits(0)
            for k in range(2):
                stored(pe, ("pT", k))
            rows_product("pp", 2, w_pp, range(2), src=pT)
            turn_rows(2, 1)
            rows_product("pp", 0, w_pp, range(2), src=pT, halves=(0,))
            logits(1)
            rows_product("pp", 0, w_pp, range(2), src=pT, halves=(1,))
            o = open_bank("pos")
            m2, m0, m1 = (msk[0:ROWS[c], c, 0:NE] for c in ORDER)
            pe.wait_ge(S["mask_ok"], 3)
            pe.matmul(o[:, NE:2 * NE], ones[0:T_S, :], m2, start=True, stop=False)
            pe.matmul(o[:, NE:2 * NE], ones[:, :], m0, start=False, stop=False)
            pe.matmul(o[:, NE:2 * NE], strict[:, :], m1, start=False, stop=True)
            pe.matmul(o[0:T_S, 2 * NE:3 * NE], strict[0:T_S, 0:T_S], m2, start=True, stop=True)
            pe.matmul(o[:, 0:NE], ones[0:T_S, :], m2, start=True, stop=False)
            pe.matmul(o[:, 0:NE], strict[:, :], m0, start=False, stop=True)
            for c in range(NCH):
                mm = pe.matmul(o[0:1, 3 * NE:4 * NE], ones[0:ROWS[c], 0:1], msk[0:ROWS[c], c, 0:NE],
                               start=(c == 0), stop=(c == NCH - 1))
            close_bank("pos", mm)
            rows_product("pp", 1, w_pp, range(2), src=pT)
            pe.wait_ge(bank_free[2], BANK_END[1][2])

            def gather(x):
                for d in range(KD):
                    for c in range(NCH):
                        for t in range(3):
                            mm = pe.matmul(bank[2][:, CAP * d:CAP * d + CAP], mbf[:, c, t, d * P:(d + 1) * P],
                                           sel[:, x, c, :], start=(c == 0 and t == 0), stop=(c == 2 and t == 2))
                mm.then_inc(S["xt_full"], 1)

            pe.wait_ge(S["m3_ok"], 3)
            pe.wait_ge(S["sel_ok"], 1)
            gather(0)
            for b in range(8):
                pe.wait_ge(bank_free[b], BANK_END[1][b])
            pe.wait_ge(S["npass_ok"], 1)
            for sem in (S["y_full"], *s_full):
                pe.sem_inc(sem, 1)
            n_pass = pe.value_load(npi[0:1, 0:1], min_val=1, max_val=PASSES)
            with pe.Fori(0, n_pass * (NE // 2)) as q:
                for x in range(2):
                    i = 2 * q + x
                    pe.wait_ge(S["up_free"], 2 * i + 1)
                    pe.wait_ge(bias_in[x], 32 * q + 32)
                    for n in range(2):
                        for hf in range(2):
                            pe.matmul(bank[n][CAP * hf:CAP * hf + CAP, :], bias_ones[part_rows[x], :],
                                      b_up3[x][:, 1024 * hf + 512 * n:1024 * hf + 512 * n + 512], start=True, stop=False)
                    pe.wait_ge(S["xt_ready"], i + 1)
                    for s in range(8):
                        if s < len(apart):
                            if x:
                                pe.wait_ge(w_full_apart[s], 32 * q + 32)
                            else:
                                pe.wait_ge(w_full[s], 16 * q + 16)
                        else:
                            pe.wait_ge(w_full[s], 16 * i + 16)
                        for n in range(2):
                            for hf in range(2):
                                mm = pe.matmul(bank[n][CAP * hf:CAP * hf + CAP, :], xT[:, x, s, :],
                                               halves(s, x)[hf][:, 512 * n:512 * n + 512],
                                               start=False, stop=(s == 7))
                            if s == 7:
                                mm.then_inc(S["up_full"], 1)
                        if s < 7:
                            mm.then_inc(S["w_used"], 1)
                    pe.wait_ge(S["sel_ok"], i + 2)
                    gather(1 - x)
                    if x == 1:
                        pe.wait_ge(S["g_ok"], i + 1)
                        pe.wait_ge(S["at_free"], 3 * q + 2)
                        for c in range(NCH):
                            mm = pe.transpose(bank[3][:, TOK[c]], gsel[0:ROWS[c], c, :], ident[0:ROWS[c], 0:ROWS[c]])
                        mm.then_inc(S["at_full"], 1)
                    pe.wait_ge(S["at_free"], 3 * q + 2 * x + 1)
                    for f in range(4):
                        if f % 2 == 0:
                            pe.wait_ge(S["act_ready"], 2 * i + 2 + f // 2)
                        mm = pe.transpose(bank[3][:, f * P:(f + 1) * P], act_h[:, f * P:(f + 1) * P], ident[:, :])
                    mm.then_inc(S["at_full"], 1)
                    pe.wait_ge(S["ysb_ok"], 2 * i + 1)
                    pe.wait_ge(S["at_free"], 3 * q + 2 * x + 2)
                    for hf in range(2):
                        pe.matmul(bank[4][CAP * hf:CAP * hf + CAP, :], bias_ones[part_rows[x], :],
                                  b_down3[x][:, 512 * hf:512 * hf + 512], start=True, stop=False)
                    for k in range(8):
                        if k % 2 == 0:
                            pe.wait_ge(w_full[8 + k // 2], 16 * i + 16)
                        for hf in range(2):
                            mm = pe.matmul(bank[4][CAP * hf:CAP * hf + CAP, :], actT[:, k % 4, k // 4, :],
                                           slot(8 + k // 2)[:, 1024 * (k % 2) + 512 * hf:1024 * (k % 2) + 512 * hf + 512],
                                           start=False, stop=(k == 7))
                        if k == 7:
                            mm.then_inc(S["y_full"], 1)
                        elif k % 2:
                            mm.then_inc(S["w_used"], 1)
                pe.wait_ge(S["ysb_ok"], 4 * q + 5)
                for j, (c, hf) in enumerate(SCATTER):
                    before = scatter_reads(j - 3) if j >= 3 else 0
                    pe.wait_ge(s_free[j % 3], S_READS[j % 3] * q + before + 1)
                    o = bank[5 + j % 3]
                    for f in ((hf,) if c < 2 else (0, 1)):
                        mm = pe.matmul(o[:, :] if c < 2 else o[T_S * f:T_S * f + T_S, :], gselT[:, TOK[c]],
                                       ysb[:, 512 * f:512 * f + 512], start=True, stop=True)
                    mm.then_inc(s_full[j % 3], 1)

            pe.wait_ge(S["moe_done"], 1)
            for c in ORDER:
                transposed(("nT", c, 0), h, c)
                transposed(("nT", c, 1), h, c, 4)
            for c in ORDER:
                stored(pe, ("nT", c, 0))
                stored(pe, ("nT", c, 1))
                if c == 2:
                    pe.wait_ge(pw_in[0], 16)
                    rows_product("pg", 2, w_pg, range(4), last=False, split=True)
                    pe.wait_ge(pw_in[1], 16)
                    rows_product("pg", 2, w_pg, range(4, 8), first=False, split=True)
                else:
                    rows_product("pg", c, w_pg)

        @block.scalar
        def _(act):
            n_done = [0]

            def step(ins):
                n_done[0] += 1
                ins.then_inc(S["ach"], 1)
                act.wait_ge(S["ach"], n_done[0])

            act.dma_start(prow[0:24, :], I["state_conv"][0].rearrange("b k n -> (b k) n")).then_inc(S["par_in"], 16)
            act.dma_start(prow[24:28, :], I["conv_w"][0]).then_inc(S["par_in"], 16)
            act.dma_start(prow[28:29, :], I["conv_b"]).then_inc(S["par_in"], 16)
            act.dma_start(prow[29:30, :], I["norm_mix_g"]).then_inc(S["par_in"], 16)
            act.dma_start(prow[30:31, 0:SSD], I["ssd_norm_g"]).then_inc(S["par_in"], 16)
            act.dma_start(prow[30:31, SSD:D], I["mlp_out_g"]).then_inc(S["par_in"], 16)
            act.dma_start(prow[31:32, :], I["norm_moe_g"]).then_inc(S["par_in"], 16)
            act.dma_start(prow[32:33, :], I["norm_ple_g"]).then_inc(S["par_in"], 16)

            def squares(scratch, src, sums, sem, n):
                if n:
                    act.wait_ge(S[sem], n)
                act.activation(scratch, src, ACT.Square, accum_out=sums).then_inc(S[sem], 1)

            act.wait_ge(S["vinit"], 1)
            act.wait_ge(x_in[0], 16)
            squares(junk_x, h[:, 0, :], ss_x[:, 0:1], "sumsq", 0)
            act.wait_ge(x_in[2], 16)
            squares(junk_x[0:T_S, :], h[0:T_S, 2, :], ss_x[0:T_S, 2:3], "sumsq", 1)
            o = filled(act, "par")
            act.wait_ge(freed("par"), 1)
            act.activation(xps[:, :, 0:3, :],
                           o[:, 0:33 * KD].rearrange("p (k n) -> p k n", k=KD)[:, :, 0:24]
                           .rearrange("p k (b j) -> p k j b", b=B_S), ACT.Copy).then_inc(freed("par"), 1)
            def store_xbc(t):
                o = filled(act, ("xbc", t))
                act.activation(xp[:, t, 3:T_PROMPT + 3], o[:, 0:T_PROMPT], ACT.Copy).then_inc(freed(("xbc", t)), 1)
                act.activation(xps[:, t, 3:, :], o[:, T_PROMPT:T].rearrange("p (b s) -> p s b", b=B_S), ACT.Copy)\
                   .then_inc(freed(("xbc", t)), 1)

            for t in (0, 1):
                store_xbc(t)
            act.wait_ge(S["dtabs"], 1)
            act.activation(dtb, dta, ACT.Exp, scale=-1.0).then_inc(S["dtexp"], 1)
            act.wait_ge(S["dtadd"], 1)
            act.activation(av, dtc, ACT.Ln).then_inc(S["dtln"], 1)
            act.wait_ge(S["pb_in"], 48)
            act.activation(aneg, pb[:, HEADS:2 * HEADS], ACT.Exp).then_inc(S["anexp"], 1)
            for t in (2, 3):
                store_xbc(t)
            for q in range(2):
                o = filled(act, ("wT", q))
                act.activation(wspT[:, 4 * q:4 * q + 4, :].rearrange("p h i -> p (h i)"), o[:, :], ACT.Copy)\
                   .then_inc(freed(("wT", q)), 1)
            act.wait_ge(S["dec_in"], 1)
            act.activation(eac, acum, ACT.Exp).then_inc(S["eac_ok"], 1)
            act.activation(dec, dec, ACT.Exp).then_inc(S["eac_ok"], 1)
            act.activation(edec, atot[:, 1, :], ACT.Exp).then_inc(S["eac_ok"], 1)
            for c in range(2):
                for g in range(GROUPS):
                    stored(act, ("acb", c, g))
                    act.activation(lmat[c][:, 4 * g:4 * g + 4, :], lmat[c][:, 4 * g:4 * g + 4, :], ACT.Exp)\
                       .then_inc(S["lexp"], 1)
            stored(act, "acb2")
            act.activation(lmat_s, lmat_s, ACT.Exp).then_inc(S["lexp"], 1)
            o = filled(act, "decs")
            act.activation(decs[:, :, :].rearrange("p t b -> p (t b)"), o[:, 0:32], ACT.Exp).then_inc(freed("decs"), 1)
            for t in range(4, 8):
                store_xbc(t)
            for n, dst in (("cvp", cvp), ("cvs", cvs)):
                for hf in range(2):
                    o = filled(act, (n, hf))
                    act.activation(dst[0:T_S, 512 * hf:512 * hf + 512], o[0:T_S, :], ACT.Copy).then_inc(freed((n, hf)), 1)
            for t in range(8):
                act.wait_ge(S["conv_ok"], 2 * t + 2)
                act.activation(xact[:, t, :], xact[:, t, :], ACT.Silu).then_inc(S["xact_ok"], 1)
            for c in range(2):
                o = filled(act, ("z", c))
                act.activation(zs[:, c, :], o[:, :], ACT.Silu).then_inc(freed(("z", c)), 1)
            o = filled(act, "zuv2")
            for n, (dst, f) in enumerate(((zs, ACT.Silu), (us, ACT.Gelu_apprx_tanh), (vs, ACT.Gelu_apprx_tanh))):
                act.activation(dst[0:T_S, 2, :], o[T_S * n:T_S * n + T_S, :], f).then_inc(freed("zuv2"), 1)
            for c in range(NCH):
                r = slice(0, ROWS[c])
                o = filled(act, ("xtm", c))
                act.activation(xs[r, c, :], o[r, :], ACT.Copy).then_inc(freed(("xtm", c)), 1)
                o = filled(act, ("btm", c))
                act.activation(btm[r, c, :, :].rearrange("p g n -> p (g n)"), o[r, 0:256], ACT.Copy)\
                   .then_inc(freed(("btm", c)), 1)

            def gelu(name, c, dst):
                o = filled(act, (name, c))
                act.activation(dst[:, c, :], o[:, :], ACT.Gelu_apprx_tanh).then_inc(freed((name, c)), 1)

            gelu("v", 0, vs)
            gelu("v", 1, vs)
            for b in range(B_S):
                if b >= 2:
                    act.wait_ge(S["h0t_used"], b - 1)
                o = filled(act, ("h0T", b))
                act.activation(h0t[:, b % 2, :], o[:, :], ACT.Copy).then_inc(freed(("h0T", b)), 1)
            o = filled(act, "hf")
            act.activation(xdt[:, 0, :], o[:, :], ACT.Copy).then_inc(freed("hf"), 1)
            gelu("u", 0, us)
            for c in range(NCH):
                r = slice(0, ROWS[c])
                act.wait_ge(S["y_ok"], c + 1)
                for g in range(GROUPS):
                    squares(junk[r, 0:256], xs[r, c, 256 * g:256 * g + 256], ss_g[r, 2 * c + g:2 * c + g + 1],
                            "ygs", 2 * c + g)
            gelu("u", 1, us)
            act.wait_ge(S["ygs"], 6)
            for n, c in enumerate(ORDER):
                r = slice(0, ROWS[c])
                act.wait_ge(S["mix_ok"], n + 1)
                squares(junk[r, :], us[r, c, :], ss_m[r, c:c + 1], "mss", n)
            jh = view(8704, D)

            def row_squares(n):
                c = ORDER[n]
                r = slice(0, ROWS[c])
                for job in ([("wo", 2)] if c == 2 else [("wo", c, 0), ("wo", c, 1)]):
                    stored(act, job)
                squares(jh[r, :], h[r, c, :], ss_o[r, c:c + 1], "hss", n)

            def part(n, k):
                c = ORDER[n]
                r = slice(0, ROWS[c])
                src, before, done = ((mn, "mn_ok", "m1_ok"), (mr, "r1_ok", "m2_ok"))[k]
                act.wait_ge(S[before], n + 1)
                act.activation(mbf[r, c, k, :], src[r, c, :], ACT.Copy).then_inc(S[done], 1)

            def gate_exp(n):
                c = ORDER[n]
                r = slice(0, ROWS[c])
                act.wait_ge(S["ngm_ok"], n + 1)
                act.activation(ex[r, c, 0:NE], lgt[r, c, 0:NE], ACT.Exp, bias=top4[r, c, 7:8]).then_inc(S["gex"], 1)

            def evacuate(tag, c, dst, f, scale=1.0):
                r = slice(0, ROWS[c])
                for hf in range(2):
                    o = filled(act, (tag, 2) if c == 2 else (tag, c, hf))
                    at = T_S * hf if c == 2 else 0
                    job = (tag, 2) if c == 2 else (tag, c, hf)
                    act.activation(dst[r, c, 512 * hf:512 * hf + 512], o[at:at + ROWS[c], :], f, scale=scale)\
                       .then_inc(freed(job), 1)

            row_squares(0)
            act.wait_ge(S["mbf_zero"], 1)
            part(0, 0)
            row_squares(1)
            part(1, 0)
            part(0, 1)
            row_squares(2)
            for k in range(2):
                o = filled(act, ("pT", k))
                act.activation(pT[:, k, :], o[:, 0:T], ACT.Copy).then_inc(freed(("pT", k)), 1)
            part(2, 0)
            evacuate("pp", 2, pp, ACT.Copy)
            gate_exp(0)
            part(1, 1)
            gate_exp(1)
            part(2, 1)
            gate_exp(2)
            evacuate("pp", 0, pp, ACT.Copy)
            evacuate("pp", 1, pp, ACT.Copy)
            act.wait_ge(S["npass_ok"], 1)
            for sem in (S["at_free"], S["ysb_ok"]):
                act.sem_inc(sem, 1)
            n_pass = act.value_load(npi[0:1, 0:1], min_val=1, max_val=PASSES)
            with act.Fori(0, n_pass * (NE // 2)) as q:
                for x in range(2):
                    i = 2 * q + x
                    act.wait_ge(S["act_ready"], 2 * i + 1)
                    for n in range(2):
                        act.wait_ge(S["g_ready"], 2 * i + 1 + n)
                        act.activation(sq[:, 256 * n:256 * n + 256], sg[:, 256 * n:256 * n + 256], ACT.Sigmoid,
                                       scale=ALPHA).then_inc(S["sig_ready"], 1)
                    act.wait_ge(s_full[1], S_JOBS[1] * q + 1)
                    if x == 1:
                        act.wait_ge(S["at_full"], 3 * q + 2)
                        act.activation(gselT, bank[3][:, 0:T], ACT.Copy).then_inc(S["at_free"], 1)
                    act.wait_ge(S["y_full"], i + 1)
                    act.wait_ge(S["at_full"], 3 * q + 2 * x + 1)
                    act.activation(actT.rearrange("p f a s -> p (f a s)"), bank[3][:, :], ACT.Copy)\
                       .then_inc(S["at_free"], 1)
                    act.wait_ge(S["y_full"], i + 2)
                    act.activation(ysb[CAP * x:CAP * x + CAP, 0:512], bank[4][0:CAP, :], ACT.Copy)\
                       .then_inc(S["ysb_ok"], 1)
            jt = view(3072, D)
            for n, c in enumerate(ORDER):
                r = slice(0, ROWS[c])
                experts_done(act, n_pass, c)
                squares(jt[r, :], h[r, c, :], ss_p[r, c:c + 1], "fss", n)
            act.wait_ge(S["rs_p_ok"], 1)
            for hf in range(2):
                half = slice(512 * hf, 512 * hf + 512)
                act.wait_ge(S["pg_sum"], hf + 1)
                act.activation(pgs[0:T_S, 2, half], pgs[0:T_S, 2, half], ACT.Sigmoid, scale=rs_p[0:T_S, 2:3])\
                   .then_inc(S["pg_sig"], 1)
            act.wait_ge(S["rs_p_ok"], 2)
            evacuate("pg", 0, pgs, ACT.Sigmoid, rs_p[:, 0:1])
            act.wait_ge(S["fss"], 3)
            for n, c in enumerate(ORDER):
                r = slice(0, ROWS[c])
                if c == 1:
                    evacuate("pg", 1, pgs, ACT.Sigmoid, rs_p[:, 1:2])
                for hf in range(2):
                    half = slice(512 * hf, 512 * hf + 512)
                    act.wait_ge(S["hfin"], 2 * n + hf + 1)
                    squares(jt[r, half], h[r, c, half], (ss_f, ss_f2)[hf][r, c:c + 1], "fin_ss", 2 * n + hf)

        @block.vector
        def _(dve):
            n_done = [0]

            def put(ins):
                n_done[0] += 1
                ins.then_inc(S["vch"], 1)
                return n_done[0]

            def after(n):
                dve.wait_ge(S["vch"], n)

            def step(ins):
                after(put(ins))

            tt, ts, stt = dve.tensor_tensor, dve.tensor_scalar, dve.scalar_tensor_tensor

            def rstd(out, sums, total, sem=None):
                w = out.shape[-1]
                v, t = nwt[:, 0, 0:w], nwt[:, 1, 0:w]
                step(ts(v, sums, 1.0 / total, EPS, ALU.mult, ALU.add))
                step(ts(out.bitcast(I32), v.bitcast(I32), -0.5, float(0x5f3759df), ALU.mult, ALU.add))
                if w == 1:
                    step(ts(v, v, -0.5, None, ALU.mult))
                for n in range(3):
                    if w == 1:
                        step(stt(t, out, v, out, ALU.mult, ALU.mult))
                    else:
                        step(stt(t, out, -0.5, out, ALU.mult, ALU.mult))
                        step(tt(t, t, v, ALU.mult))
                    last = stt(out, t, 1.5, out, ALU.add, ALU.mult)
                    if sem and n == 2:
                        last.then_inc(S[sem], 1)
                    else:
                        step(last)

            step(dve.memset(stat[:, :, :], 0.0))
            step(dve.memset(gstat[:, :, :], 0.0))
            step(dve.memset(mv[:, :, :], 0.0))
            dve.memset(small[:, :, :], 0.0).then_inc(S["vinit"], 1)

            dve.wait_ge(S["vinit"], 1)
            dve.wait_ge(x_in[1], 16)
            step(dve.tensor_tensor_reduce(view(0, D), h[:, 1, :], h[:, 1, :], 1.0, 0.0, ALU.mult, ALU.add, ss_x[:, 1:2]))
            dve.wait_ge(S["sumsq"], 2)
            rstd(rs_x, ss_x, D)
            for c in range(NCH):
                r = slice(0, ROWS[c])
                ts(xn[r, c, :], h[r, c, :], rs_x[r, c:c + 1], None, ALU.mult).then_inc(S["xn_ok"], 1)
            o = filled(dve, "par")
            dve.tensor_copy(pf[:, :, :], o[:, 0:33 * KD].rearrange("p (k n) -> p k n", k=KD)[:, :, 24:33])\
               .then_inc(freed("par"), 1)
            dve.wait_ge(freed("par"), 1)

            def turned(tag, g, order):
                for c, hf in order:
                    o = filled(dve, (tag, c, hf))
                    n = ROWS[c]
                    tt(aT[:, 4 * hf:4 * hf + 4, TOK[c]], o[:, 0:4 * n].rearrange("p (k t) -> p k t", k=4),
                       over(pf[:, 4 * hf:4 * hf + 4, g], [P, 4, n]), ALU.mult).then_inc(freed((tag, c, hf)), 1)

            turned("xT", 5, CH)
            def convolve(t):
                stored(dve, ("xbc", t))
                outs = (xact[:, t, 0:T_PROMPT], xact[:, t, T_PROMPT:].rearrange("p (b s) -> p s b", b=B_S))

                def tap(n, j):
                    return xp[:, t, j:j + T_PROMPT] if n == 0 else xps[:, t, j:j + L_S, :]

                last = [put(ts(outs[n], tap(n, 0), pf[:, t, 0:1], pf[:, t, 4:5], ALU.mult, ALU.add)) for n in range(2)]
                for j in range(1, 4):
                    for n in range(2):
                        after(last[n])
                        ins = stt(outs[n], tap(n, j), pf[:, t, j:j + 1], outs[n], ALU.mult, ALU.add)
                        if j == 3:
                            ins.then_inc(S["conv_ok"], 1)
                        else:
                            last[n] = put(ins)

            stored(dve, "par")
            dve.wait_ge(S["pads"], 1)
            for t in (0, 1):
                convolve(t)
            dve.wait_ge(S["pb_in"], 48)
            o = filled(dve, "dt")
            for c in range(NCH):
                r = slice(0, ROWS[c])
                tt(dtr[r, c, :], o[r, 8 * c:8 * c + 8], pb[r, 0:HEADS], ALU.add).then_inc(freed("dt"), 1)
            stored(dve, "dt")
            stt(dta, dtr, -1.0, dtr, ALU.mult, ALU.max).then_inc(S["dtabs"], 1)
            dve.wait_ge(S["dtexp"], 1)
            ts(dtc, dtb, 1.0, None, ALU.add).then_inc(S["dtadd"], 1)
            dve.wait_ge(S["dtadd"], 1)
            step(ts(dta, dtc, -1.0, None, ALU.add))
            dve.wait_ge(S["dtln"], 1)
            step(ts(dtc, dta, 0.0, None, ALU.is_equal))
            step(tt(dta, dta, dtc, ALU.add))
            step(tt(av, av, dtc, ALU.add))
            step(dve.reciprocal(dta, dta))
            step(tt(dta, dta, av, ALU.mult))
            step(tt(dta, dta, dtb, ALU.mult))
            step(stt(dt, dtr, 0.0, dta, ALU.max, ALU.add))
            dve.wait_ge(S["anexp"], 1)
            stt(av, dt, -1.0, aneg.unsqueeze(1).to_broadcast([P, NCH, HEADS]), ALU.mult, ALU.mult).then_inc(S["a_ok"], 1)
            dve.wait_ge(S["a_ok"], 1)
            dve.tensor_copy(hs3(aex[0:T_S, :]), over(av[0:T_S, 2, :], [T_S, HEADS, HD])).then_inc(S["aex_ok"], 1)
            for t in (2, 3):
                convolve(t)
            o = filled(dve, "bT")
            dve.tensor_copy(bsp[:, :], o[:, 0:MHEADS]).then_inc(freed("bT"), 1)
            o = filled(dve, "acum")
            dve.tensor_copy(acum[:, 0:2, :].rearrange("p c h -> p (c h)"), o[:, 0:16]).then_inc(freed("acum"), 1)
            dve.tensor_copy(small[0:T_S, 6:8, 16:24], o[0:T_S, 16:32].rearrange("p (a h) -> p a h", a=2))\
               .then_inc(freed("acum"), 1)
            stored(dve, "acum")
            for c in range(2):
                for g in range(GROUPS):
                    o = filled(dve, ("acb", c, g))
                    rows = o[:, :].rearrange("p (h i) -> p h i", h=HPG)
                    dve.tensor_copy(atot[:, c, 4 * g:4 * g + 4], rows[:, :, P - 1]).then_inc(freed(("acb", c, g)), 1)
                    for j in range(HPG):
                        hh = HPG * g + j
                        stt(lmat[c][:, hh, :], rows[:, j, :], acum[:, c, hh:hh + 1], negm[:, :],
                            ALU.subtract, ALU.add).then_inc(freed(("acb", c, g)), 1)
            o = filled(dve, "acb2")
            for hh in range(HEADS):
                stt(lmat_s[:, hh, :], o[0:T_S, hh * T_S:(hh + 1) * T_S], acum[0:T_S, 2, hh:hh + 1], negm_s[:, :],
                    ALU.subtract, ALU.add).then_inc(freed("acb2"), 1)
            for c in range(2):
                for g in range(GROUPS):
                    stored(dve, ("acb", c, g))
            tt(dec, atot, acum, ALU.subtract).then_inc(S["dec_in"], 1)
            for t in range(4, 8):
                convolve(t)
            o = filled(dve, "rep")
            for_b = o[0:T_S, 0:32].rearrange("p (h i) -> p h i", h=MHEADS).unsqueeze(2).to_broadcast([T_S, MHEADS, B_S, L_S])
            tt(wsps[0:T_S, :, :, :], for_b, block_s[:, :].rearrange("p (b s) -> p b s", b=B_S).unsqueeze(1)
               .to_broadcast([T_S, MHEADS, B_S, L_S]), ALU.mult).then_inc(freed("rep"), 1)
            dve.tensor_copy(bss[:, :], o[0:T_S, 32:40]).then_inc(freed("rep"), 1)
            dve.wait_ge(S["xact_ok"], 8)
            for g in range(GROUPS):
                tt(cmask[:, g, :, :], xact[:, 6 + g, T_PROMPT:].unsqueeze(1).to_broadcast([P, B_S, T_S]), seqm, ALU.mult)\
                    .then_inc(S["cmask_ok"], 1)
            dve.wait_ge(S["lexp"], 5)
            for c in range(NCH):
                o = filled(dve, ("cb", c))
                for g in range(GROUPS):
                    n = ROWS[c]
                    part = lmat[c][:, 4 * g:4 * g + 4, :] if c < 2 else lmat_s[:, 4 * g:4 * g + 4, :]
                    tt(part, part, o[0:n, g * P:g * P + n].unsqueeze(1).to_broadcast([n, HPG, n]), ALU.mult)\
                        .then_inc(freed(("cb", c)), 1)
            dve.wait_ge(S["eac_ok"], 3)
            dve.wait_ge(S["cv_out"], 16 * L_S)
            for c in range(NCH):
                r, n = slice(0, ROWS[c]), ROWS[c]
                stored(dve, ("xtm", c))
                step(tt(hs3(xdt[r, c, :]), hs3(xs[r, c, :]), over(dt[r, c, :], [n, HEADS, HD]), ALU.mult))
                tt(hs3(xdtd[r, c, :]), hs3(xdt[r, c, :]), over(dec[r, c, :], [n, HEADS, HD]), ALU.mult)\
                    .then_inc(S["xdtd_ok"], 1)
                n_skip = put(tt(hs3(xs[r, c, :]), hs3(xs[r, c, :]), over(pb[r, 16:24], [n, HEADS, HD]), ALU.mult))
            o = filled(dve, ("st", 0))
            dve.tensor_copy(hs1, o[:, :]).then_inc(freed(("st", 0)), 1)
            stored(dve, ("st", 0))
            step(tt(hs3(hs2), hs3(hs1), over(edec, [P, HEADS, HD]), ALU.mult))
            o = filled(dve, ("st", 1))
            tt(hs2, hs2, o[:, :], ALU.add).then_inc(freed(("st", 1)), 1)
            stored(dve, ("btm", 2))
            for g in range(GROUPS):
                tt(bmask[0:T_S, g, :, :], btm[0:T_S, 2, g, :].unsqueeze(1).to_broadcast([T_S, B_S, N_ST]),
                   over(seq_s[:, :], [T_S, B_S, N_ST]), ALU.mult).then_inc(S["bmask_ok"], 1)
            after(n_skip)

            def add_diagonal(c):
                r = slice(0, ROWS[c])
                o = filled(dve, ("yd", c))
                tt(xs[r, c, :], xs[r, c, :], o[r, :], ALU.add).then_inc(freed(("yd", c)), 1)
                stored(dve, ("yd", c))

            def gated_y(c):
                r = slice(0, ROWS[c])
                if c == 1:
                    o = filled(dve, "yo1")
                    tt(hs3(yoff), hs3(o[:, :]), over(eac[:, 1, :], [P, HEADS, HD]), ALU.mult).then_inc(freed("yo1"), 1)
                    stored(dve, "yo1")
                if c == 2:
                    o = filled(dve, "yos")
                    _, _, before, _ = PS["yos"]
                    for g in range(GROUPS):
                        dve.tensor_copy(yoff[0:T_S, 256 * g:256 * g + 256], o[T_S * g:T_S * g + T_S, 0:256])\
                            .then_inc(freed("yos"), 1)
                    for g in range(GROUPS):
                        dve.wait_ge(freed("yos"), before + 1 + g)
                        part = yoff[0:T_S, 256 * g:256 * g + 256]
                        tt(part, part, o[T_S * (2 + g):T_S * (3 + g), 0:256], ALU.add).then_inc(freed("yos"), 1)
                    stored(dve, "yos")
                    step(tt(hs3(yoff[0:T_S, :]), hs3(yoff[0:T_S, :]), over(eac[0:T_S, 2, :], [T_S, HEADS, HD]), ALU.mult))
                if c:
                    step(tt(xs[r, c, :], xs[r, c, :], yoff[r, :], ALU.add))
                stored(dve, ("z", c) if c < 2 else "zuv2")
                tt(xs[r, c, :], xs[r, c, :], zs[r, c, :], ALU.mult).then_inc(S["y_ok"], 1)

            add_diagonal(0)
            gated_y(0)
            add_diagonal(1)
            gated_y(1)
            add_diagonal(2)
            for c in ORDER:
                r = slice(0, ROWS[c])
                stored(dve, ("v", c) if c < 2 else "zuv2")
                n = put(dve.bn_stats(bn[r, c, :], vs[r, c, :]))
            after(n)
            for c in range(NCH):
                r = slice(0, ROWS[c])
                n = put(dve.bn_aggr(mv[r, c, :], bn[r, c, :]))
            after(n)
            rstd(rs_v, mv[:, :, 1], 1)
            dve.wait_ge(S["vgb_in"], 32)
            for c in ORDER:
                r = slice(0, ROWS[c])
                n = put(ts(vs[r, c, :], vs[r, c, :], mv[r, c, 0:1], rs_v[r, c:c + 1], ALU.subtract, ALU.mult))
            after(n)
            for c in ORDER:
                r = slice(0, ROWS[c])
                n = put(tt(vs[r, c, :], vs[r, c, :], vgb[r, 0, :], ALU.mult))
            after(n)
            for c in ORDER:
                r = slice(0, ROWS[c])
                tt(vs[r, c, :], vs[r, c, :], vgb[r, 1, :], ALU.add).then_inc(S["vn_ok"], 1)
            gated_y(2)
            def new_states(ts):
                for t in ts:
                    for bh in range(2):
                        o = filled(dve, ("ns", t, bh))
                        for j in range(4):
                            b = 4 * bh + j
                            stt(h0[:, b, t, :], h0[:, b, t, :], decs[:, t, b:b + 1], o[:, j * P:(j + 1) * P],
                                ALU.mult, ALU.add).then_inc(freed(("ns", t, bh)), 1)

            dve.wait_ge(S["h0_in"], 16)
            stored(dve, "decs")
            new_states((0, 1))
            dve.wait_ge(S["ygs"], 6)
            rstd(rs_g, ss_g, 256)
            for c in ORDER:
                r = slice(0, ROWS[c])
                for g in range(GROUPS):
                    ts(xs[r, c, 256 * g:256 * g + 256], xs[r, c, 256 * g:256 * g + 256],
                       rs_g[r, 2 * c + g:2 * c + g + 1], None, ALU.mult).then_inc(S["yn_ok"], 1)
            new_states((2, 3))
            turned("cat", 6, [(c, 0) for c in ORDER])
            for c in ORDER:
                r, n = slice(0, ROWS[c]), ROWS[c]
                bs = bsp[:, :] if c < 2 else bss[:, :]
                o = filled(dve, ("sp", c))
                dve.wait_ge(S["y_ok"], 3)
                tt(hs3(zs[r, c, :]), hs3(o[r, :]), over(bs, [n, MHEADS, MHD]), ALU.add).then_inc(freed(("sp", c)), 1)
                stored(dve, ("sp", c))
                stored(dve, ("u", c) if c < 2 else "zuv2")
                tt(us[r, c, :], us[r, c, :], zs[r, c, :], ALU.mult).then_inc(S["mix_ok"], 1)
            for n, c in enumerate(ORDER):
                r = slice(0, ROWS[c])
                dve.wait_ge(S["mss"], n + 1)
                rstd(rs_m[:, c:c + 1], ss_m[:, c:c + 1], MLP)
                ts(us[r, c, :], us[r, c, :], rs_m[r, c:c + 1], None, ALU.mult).then_inc(S["m_ok"], 1)
            turned("cat", 6, [(c, 1) for c in ORDER])
            for c in ORDER:
                stored(dve, ("cat", c, 1))
            dve.memset(npf[0:1, 7:8], 0.0).then_inc(S["mix_done"], 1)

            def residual(n):
                c = ORDER[n]
                r = slice(0, ROWS[c])
                for m in range(2 if c == 2 else 1):
                    for hf in range(2):
                        job = ("wo", 2) if c == 2 else ("wo", c, hf)
                        at = T_S * (2 * m + hf) if c == 2 else 0
                        o = filled(dve, job)
                        if m:
                            dve.wait_ge(freed(job), PS[job][2] + 1 + hf)
                        part = h[r, c, 512 * hf:512 * hf + 512]
                        tt(part, part, o[at:at + ROWS[c], :], ALU.add).then_inc(freed(job), 1)

            def normalise(n):
                c = ORDER[n]
                r = slice(0, ROWS[c])
                dve.wait_ge(S["hss"], n + 1)
                rstd(rs_o[:, c:c + 1], ss_o[:, c:c + 1], D)
                ts(mn[r, c, :], h[r, c, :], rs_o[r, c:c + 1], None, ALU.mult).then_inc(S["mn_ok"], 1)

            def rest(n, k):
                c = ORDER[n]
                r = slice(0, ROWS[c])
                if k == 1:
                    dve.wait_ge(S["m1_ok"], n + 1)
                    tt(mr[r, c, :], mn[r, c, :], mbf[r, c, 0, :], ALU.subtract).then_inc(S["r1_ok"], 1)
                else:
                    dve.wait_ge(S["m2_ok"], n + 1)
                    tt(mbf[r, c, 2, :], mr[r, c, :], mbf[r, c, 1, :], ALU.subtract).then_inc(S["m3_ok"], 1)

            def choose(n):
                c = ORDER[n]
                r = slice(0, ROWS[c])
                o = filled(dve, ("lg", c))
                tt(lgt[r, c, 0:NE], o[r, 0:NE], brow[r, :], ALU.add).then_inc(freed(("lg", c)), 1)
                stored(dve, ("lg", c))
                step(dve.max(top8[r, c, :], lgt[r, c, 0:NE]))
                step(dve.tensor_copy(top4[r, c, 0:4], top8[r, c, 0:4]))
                step(dve.match_replace(mrep[r, c, :], top4[r, c, :], lgt[r, c, :], -BIG))
                tt(msk[r, c, 0:NE], mrep[r, c, 0:NE], lgt[r, c, 0:NE], ALU.not_equal).then_inc(S["mask_ok"], 1)
                ts(top4[r, c, 7:8], top8[r, c, 0:1], -1.0, None, ALU.mult).then_inc(S["ngm_ok"], 1)

            dve.wait_ge(S["v_out"], 16)
            dve.wait_ge(S["hf_out"], 16)
            residual(0)
            normalise(0)
            residual(1)
            turned("mT", 7, [(2, 0), (2, 1)])
            normalise(1)
            rest(0, 1)
            dve.wait_ge(S["brow_in"], 16)
            dve.wait_ge(S["tables"], 6)
            choose(0)
            rest(0, 2)
            residual(2)
            turned("mT", 7, [(0, 0), (0, 1)])
            normalise(2)
            rest(1, 1)
            turned("mT", 7, [(1, 0), (1, 1)])
            choose(1)
            rest(2, 1)
            choose(2)
            rest(1, 2)
            rest(2, 2)
            dve.wait_ge(S["mask_ok"], 3)
            o = filled(dve, "pos")
            for c in range(NCH):
                r = slice(0, ROWS[c])
                stt(prk[r, c, 0:NE], o[r, NE * c:NE * c + NE], 1.0, msk[r, c, 0:NE], ALU.add, ALU.mult)\
                    .then_inc(freed("pos"), 1)
            dve.tensor_reduce(npf[0:1, 0:1], o[0:1, 3 * NE:4 * NE], AX_X, ALU.max).then_inc(freed("pos"), 1)
            stored(dve, "pos")

            def places(p):
                return put(ts(pos_t[:, :, NE * p:NE * p + NE], prk[:, :, 0:NE], float(-1 - CAP * p), None, ALU.add))

            def pick(x, i):
                at = pos_t[:, :, bass.ds(i, 1)].to_broadcast([P, NCH, CAP])
                tt(sel[:, x, :, :], iota[:, :].unsqueeze(1).to_broadcast([P, NCH, CAP]), at, ALU.is_equal)\
                    .then_inc(S["sel_ok"], 1)

            after(places(0))
            pick(0, 0)
            step(ts(npf[0:1, 1:PASSES], thr[:, :], npf[0:1, 0:1], None, ALU.is_lt))
            step(dve.tensor_reduce(npf[0:1, 5:6], npf[0:1, 1:PASSES], AX_X, ALU.add))
            step(ts(npf[0:1, 6:7], npf[0:1, 5:6], 1.0, None, ALU.add))
            dve.tensor_copy(npi[:, :], npf[0:1, 6:7]).then_inc(S["npass_ok"], 1)
            for n, c in enumerate(ORDER):
                r = slice(0, ROWS[c])
                dve.wait_ge(S["gex"], n + 1)
                step(dve.tensor_tensor_reduce(gat[r, c, 0:NE], ex[r, c, 0:NE], msk[r, c, 0:NE], 1.0, 0.0,
                                              ALU.mult, ALU.add, gsum[r, c:c + 1]))
                step(dve.reciprocal(grec[r, c:c + 1], gsum[r, c:c + 1]))
                step(ts(gat[r, c, 0:NE], gat[r, c, 0:NE], grec[r, c:c + 1], None, ALU.mult))
            for p in range(PASSES):
                if p:
                    places(p)
                n = put(dve.tensor_copy(gate_t[:, :, NE * p:NE * p + NE], gat[:, :, 0:NE]))
            after(n)

            def gathered(x, n):
                dve.wait_ge(S["xt_full"], n)
                tt(xT[:, x, :, :], bank[2][:, :].rearrange("p (k s) -> p k s", k=KD), over(pf[:, :, 7], [P, KD, CAP]),
                   ALU.mult).then_inc(S["xt_ready"], 1)

            gathered(0, 1)
            dve.wait_ge(S["npass_ok"], 1)
            dve.wait_ge(S["tables"], 7)
            for sem in (S["up_free"], S["act_ready"], *s_free):
                dve.sem_inc(sem, 1)
            n_pass = dve.value_load(npi[0:1, 0:1], min_val=1, max_val=PASSES)
            with dve.Fori(0, n_pass * (NE // 2)) as q:
                for x in range(2):
                    i = 2 * q + x
                    pick(1 - x, i + 1)
                    dve.wait_ge(S["sel_ok"], i + 1)
                    tt(gsel[:, :, CAP * x:CAP * x + CAP], sel[:, x, :, :],
                       gate_t[:, :, bass.ds(i, 1)].to_broadcast([P, NCH, CAP]), ALU.mult).then_inc(S["g_ok"], 1)
                    for n in range(2):
                        dve.wait_ge(S["up_full"], 2 * i + 1 + n)
                        cols = bank[n][:, :].rearrange("p (f two) -> p f two", two=2)
                        half = slice(256 * n, 256 * n + 256)
                        ts(sg[:, half], cols[:, :, 0], LIMIT, None, ALU.min).then_inc(S["g_ready"], 1)
                        ts(sl[:, half], cols[:, :, 1], LIMIT, -LIMIT, ALU.min, ALU.max).then_inc(S["up_free"], 1)
                    for n in range(2):
                        half = slice(256 * n, 256 * n + 256)
                        dve.wait_ge(S["up_free"], 2 * i + 2 + n)
                        stt(sl[:, half], sl[:, half], 1.0, sg[:, half], ALU.add, ALU.mult).then_inc(S["gl_ok"], 1)
                        dve.wait_ge(S["gl_ok"], 2 * i + 1 + n)
                        dve.wait_ge(S["sig_ready"], 2 * i + 1 + n)
                        tt(act_h[:, half], sl[:, half], sq[:, half], ALU.mult).then_inc(S["act_ready"], 1)
                    gathered(1 - x, i + 2)
                    dve.wait_ge(S["y_full"], i + 2)
                    dve.tensor_copy(ysb[CAP * x:CAP * x + CAP, 512:1024], bank[4][CAP:2 * CAP, :]).then_inc(S["ysb_ok"], 1)
                for j, (c, hf) in enumerate(SCATTER):
                    r = slice(0, ROWS[c])
                    dve.wait_ge(s_full[j % 3], S_JOBS[j % 3] * q + j // 3 + 2)
                    for n, f in enumerate((hf,) if c < 2 else (0, 1)):
                        part = h[r, c, 512 * f:512 * f + 512]
                        at = T_S * f if c == 2 else 0
                        before = scatter_reads(j - 3) if j >= 3 else 0
                        dve.wait_ge(s_free[j % 3], S_READS[j % 3] * q + before + n + 1)
                        tt(part, part, bank[5 + j % 3][at:at + ROWS[c], :], ALU.add).then_inc(s_free[j % 3], 1)
            for j in range(3):
                dve.wait_ge(s_free[j], n_pass * (NE // 2 * S_READS[j]) + 1)
            dve.memset(npf[0:1, 7:8], 0.0).then_inc(S["moe_done"], 1)
            turned("nT", 8, [(c, hf) for c in ORDER for hf in range(2)])
            dve.wait_ge(S["fss"], 1)
            rstd(rs_p[:, 2:3], ss_p[:, 2:3], D, "rs_p_ok")
            dve.wait_ge(S["fss"], 3)
            dve.wait_ge(S["rs_p_ok"], 1)
            rstd(rs_p[:, 0:2], ss_p[:, 0:2], D, "rs_p_ok")

            def gated(n):
                c = ORDER[n]
                r = slice(0, ROWS[c])
                for hf in range(2):
                    half = slice(512 * hf, 512 * hf + 512)
                    if c == 2:
                        dve.wait_ge(S["pg_sig"], hf + 1)
                    else:
                        stored(dve, ("pg", c, hf))
                    step(tt(pgs[r, c, half], pgs[r, c, half], pp[r, c, half], ALU.mult))
                    tt(h[r, c, half], h[r, c, half], pgs[r, c, half], ALU.add).then_inc(S["hfin"], 1)

            def final(n):
                c = ORDER[n]
                r = slice(0, ROWS[c])
                dve.wait_ge(S["fin_ss"], 2 * n + 2)
                step(tt(ss_f[:, c:c + 1], ss_f[:, c:c + 1], ss_f2[:, c:c + 1], ALU.add))
                rstd(rs_f[:, c:c + 1], ss_f[:, c:c + 1], D)
                for hf in range(2):
                    half = slice(512 * hf, 512 * hf + 512)
                    stt(yout[r, c, half], h[r, c, half], rs_f[r, c:c + 1], gfin[r, half], ALU.mult, ALU.mult)\
                        .then_inc(S["yo_ok"], 1)

            o = filled(dve, ("pg", 2))
            for hf in range(2):
                half = slice(512 * hf, 512 * hf + 512)
                dve.tensor_copy(pgs[0:T_S, 2, half], o[T_S * hf:T_S * hf + T_S, :]).then_inc(freed(("pg", 2)), 1)
            for hf in range(2):
                half = slice(512 * hf, 512 * hf + 512)
                dve.wait_ge(freed(("pg", 2)), PS[("pg", 2)][2] + 1 + hf)
                tt(pgs[0:T_S, 2, half], pgs[0:T_S, 2, half], o[T_S * (2 + hf):T_S * (3 + hf), :], ALU.add)\
                    .then_inc(S["pg_sum"], 1)
            gated(0)
            dve.wait_ge(S["gf_in"], 16)
            final(0)
            gated(1)
            final(1)
            gated(2)
            final(2)


_INS = ["x_prompt", "x_sample", "state_ssm", "state_conv", "p_prompt", "p_sample", "norm_mix_g", "w_in", "conv_w",
        "conv_b", "dt_bias", "a_log", "d_skip", "ssd_norm_g", "v_norm_g", "v_norm_b", "w_spatial", "b_spatial",
        "mlp_out_g", "w_out", "norm_moe_g", "w_router", "b_router", "w_up", "b_up", "w_down", "b_down", "norm_ple_g",
        "w_ple_gate", "w_ple_proj", "norm_final_g"]
_OUTS = [("y_prompt", (1, T_PROMPT, D)), ("y_sample", (B_S, L_S, D)),
         ("new_ssm_prompt", (1, 1, HEADS, HD, N_ST)), ("new_conv_prompt", (1, 1, 3, CONV)),
         ("new_ssm_sample", (1, B_S, HEADS, HD, N_ST)), ("new_conv_sample", (1, B_S, 3, CONV)),
         ("new_chunk_v_sample", (1, B_S, L_S, MLP))]


def kernel(**inputs):
    import numpy as _np
    import concourse.bacc as _bacc
    from concourse.bass_utils import run_bass_kernel_spmd as _run

    nc = _bacc.Bacc("TRN2", target_bir_lowering=False, num_devices=1)
    arrays, ins, outs = {}, {}, {}
    for name in _INS:
        a = _np.ascontiguousarray(inputs[name])
        arrays[f"in_{name}_dram"] = a
        ins[name] = nc.dram_tensor(f"in_{name}_dram", a.shape, mybir.dt.from_np(a.dtype), kind="ExternalInput").ap()
    for name, shape in _OUTS:
        outs[name] = nc.dram_tensor(f"out_{name}_dram", shape, F32, kind="ExternalOutput").ap()
    build(nc, ins, outs)
    r = _run(nc, [arrays], core_ids=[0])
    return tuple(r.results[0][f"out_{name}_dram"] for name, _ in _OUTS)
```
